# Optimizing a Trainium2 kernel written in Bass

```python
import jax, jax.numpy as jnp
from jax import lax
import numpy as np
import math

D_MODEL = 1024
BATCH = 1
SEQ = 256
DEPTH = 2

CHUNK = 64
D_CONV = D_MODEL // 4
CONV_WIDTH = 31
SB_HEAD_DIM = 64
D_SB = D_MODEL // 2
N_SB_HEADS = D_SB // SB_HEAD_DIM
RET_HEAD_DIM = 64
D_RET = D_MODEL // 4
N_RET_HEADS = D_RET // RET_HEAD_DIM
D_MIX = D_CONV + D_SB + D_RET
D_IN_PROJ = 2 * D_CONV + 3 * D_SB + 4 * D_RET
D_FF = ((8 * D_MODEL // 3 + 127) // 128) * 128
Q_BLOCK = 128
ROPE_BASE = 10000.0
EPS = 1e-6


def rms_norm(x, g):
    xf = x.astype(jnp.float32)
    y = xf * lax.rsqrt(jnp.mean(xf * xf, axis=-1, keepdims=True) + EPS)
    return (y * g.astype(jnp.float32)).astype(x.dtype)

def layer_norm(x, g, b):
    xf = x.astype(jnp.float32)
    mu = jnp.mean(xf, axis=-1, keepdims=True)
    xc = xf - mu
    var = jnp.mean(xc * xc, axis=-1, keepdims=True)
    return (xc * lax.rsqrt(var + EPS) * g.astype(jnp.float32) + b.astype(jnp.float32)).astype(x.dtype)

def swiglu(h, w_in, w_out):
    gate, up = jnp.split(h @ w_in, 2, axis=-1)
    return (jax.nn.silu(gate) * up) @ w_out

def conv_module(u, conv_w, conv_b, ln_g, ln_b):
    a, b = jnp.split(u, 2, axis=-1)
    v = a * jax.nn.sigmoid(b)
    v = jnp.pad(v, ((0, 0), (CONV_WIDTH - 1, 0), (0, 0)))
    y = lax.conv_general_dilated(
        v, conv_w[:, None, :].astype(v.dtype), window_strides=(1,), padding="VALID",
        dimension_numbers=("NWC", "WIO", "NWC"), feature_group_count=D_CONV)
    y = y + conv_b
    return jax.nn.silu(layer_norm(y, ln_g, ln_b))

def stick_breaking(q, k, v):
    B, S, H, Dh = q.shape
    nb = S // Q_BLOCK
    qb = q.reshape(B, nb, Q_BLOCK, H, Dh).transpose(1, 0, 2, 3, 4)
    kpos = jnp.arange(S)
    scale = Dh ** -0.5

    def block(args):
        qi, i = args
        z = jnp.einsum("bqhd,bkhd->bhqk", qi, k,
                       preferred_element_type=jnp.float32) * scale
        qpos = i * Q_BLOCK + jnp.arange(Q_BLOCK)
        mask = kpos[None, :] < qpos[:, None]
        log_beta = jax.nn.log_sigmoid(z)
        log_not = jnp.where(mask, jax.nn.log_sigmoid(-z), 0.0)
        remain = lax.cumsum(log_not, axis=3, reverse=True) - log_not
        w = jnp.where(mask, jnp.exp(log_beta + remain), 0.0)
        return jnp.einsum("bhqk,bkhd->bqhd", w.astype(v.dtype), v)

    out = lax.map(block, (qb, jnp.arange(nb)))
    return out.transpose(1, 0, 2, 3, 4).reshape(B, S, H, Dh)

def rotary(x, pos):
    half = x.shape[-1] // 2
    inv = 1.0 / (ROPE_BASE ** (jnp.arange(half, dtype=jnp.float32) / half))
    ang = pos.astype(jnp.float32)[:, None] * inv[None, :]
    cos = jnp.cos(ang)[None, :, None, :]
    sin = jnp.sin(ang)[None, :, None, :]
    x1 = x[..., :half].astype(jnp.float32)
    x2 = x[..., half:].astype(jnp.float32)
    return jnp.concatenate([x1 * cos - x2 * sin, x1 * sin + x2 * cos], axis=-1).astype(x.dtype)

def retention(q, k, v):
    B, S, H, Dh = q.shape
    nc = S // CHUNK
    log_gamma = jnp.log1p(-jnp.exp2(-5.0 - jnp.arange(H, dtype=jnp.float32)))
    qc = (q * (Dh ** -0.5)).reshape(B, nc, CHUNK, H, Dh)
    kc = k.reshape(B, nc, CHUNK, H, Dh)
    vc = v.reshape(B, nc, CHUNK, H, Dh)
    idx = jnp.arange(CHUNK, dtype=jnp.float32)
    d_intra = jnp.exp(log_gamma[:, None, None] * jnp.abs(idx[:, None] - idx[None, :]))
    scores = jnp.einsum("bnihd,bnjhd->bnhij", qc, kc,
                        preferred_element_type=jnp.float32) * d_intra
    y_intra = jnp.einsum("bnhij,bnjhe->bnihe", scores, vc.astype(jnp.float32))
    k_decay = jnp.exp(log_gamma[None, :] * (CHUNK - 1 - idx)[:, None])
    kv = jnp.einsum("bnjhd,jh,bnjhe->bnhde", kc.astype(jnp.float32), k_decay,
                    vc.astype(jnp.float32))
    chunk_decay = jnp.exp(log_gamma * CHUNK)[None, :, None, None]

    def step(state, kv_n):
        return chunk_decay * state + kv_n, state

    _, s_prev = lax.scan(step, jnp.zeros((B, H, Dh, Dh), jnp.float32),
                         kv.transpose(1, 0, 2, 3, 4))
    s_prev = s_prev.transpose(1, 0, 2, 3, 4)
    q_decay = jnp.exp(log_gamma[None, :] * (idx + 1.0)[:, None])
    y_cross = jnp.einsum("bnihd,ih,bnhde->bnihe", qc.astype(jnp.float32), q_decay, s_prev)
    return (y_intra + y_cross).reshape(B, S, H, Dh)

def head_norm(y, g):
    B, S, H, Dh = y.shape
    mu = jnp.mean(y, axis=-1, keepdims=True)
    yc = y - mu
    var = jnp.mean(yc * yc, axis=-1, keepdims=True)
    return (yc * lax.rsqrt(var + EPS)).reshape(B, S, H * Dh) * g.astype(jnp.float32)

def hybrid_mixer(h, w_in, conv_w, conv_b, conv_ln_g, conv_ln_b, ret_norm_g, w_out, pos):
    B, S, _ = h.shape
    o1 = 2 * D_CONV
    o2 = o1 + D_SB
    o3 = o2 + D_SB
    o4 = o3 + D_SB
    o5 = o4 + D_RET
    o6 = o5 + D_RET
    o7 = o6 + D_RET
    u_conv, q_sb, k_sb, v_sb, q_r, k_r, v_r, g_r = jnp.split(
        h @ w_in, [o1, o2, o3, o4, o5, o6, o7], axis=-1)
    y_conv = conv_module(u_conv, conv_w, conv_b, conv_ln_g, conv_ln_b)
    sb = lambda t: t.reshape(B, S, N_SB_HEADS, SB_HEAD_DIM)
    y_sb = stick_breaking(sb(q_sb), sb(k_sb), sb(v_sb)).reshape(B, S, D_SB)
    rt = lambda t: t.reshape(B, S, N_RET_HEADS, RET_HEAD_DIM)
    y_r = retention(rotary(rt(q_r), pos), rotary(rt(k_r), pos), rt(v_r))
    y_r = jax.nn.silu(g_r.astype(jnp.float32)) * head_norm(y_r, ret_norm_g)
    y = jnp.concatenate([y_conv, y_sb, y_r.astype(h.dtype)], axis=-1)
    return y @ w_out

def first_inputs(seed: int = 0) -> dict:
    key = jax.random.key(seed)
    ks = jax.random.split(key, 20)
    f32 = jnp.float32
    nrm = lambda k, shape, scale: jax.random.normal(k, shape, f32) * scale
    gain = lambda k, shape: 1.0 + 0.02 * jax.random.normal(k, shape, f32)
    return {
        "x": jax.random.normal(ks[0], (BATCH, SEQ, D_MODEL), f32),
        "ffn1_norm": gain(ks[1], (DEPTH, D_MODEL)),
        "ffn1_w_in": nrm(ks[2], (DEPTH, D_MODEL, 2 * D_FF), D_MODEL ** -0.5),
        "ffn1_w_out": nrm(ks[3], (DEPTH, D_FF, D_MODEL), D_FF ** -0.5),
        "mix_norm": gain(ks[4], (DEPTH, D_MODEL)),
        "mix_w_in": nrm(ks[5], (DEPTH, D_MODEL, D_IN_PROJ), D_MODEL ** -0.5),
        "conv_w": nrm(ks[6], (DEPTH, CONV_WIDTH, D_CONV), CONV_WIDTH ** -0.5),
        "conv_b": nrm(ks[7], (DEPTH, D_CONV), 0.02),
        "conv_ln_g": gain(ks[8], (DEPTH, D_CONV)),
        "conv_ln_b": nrm(ks[9], (DEPTH, D_CONV), 0.02),
        "ret_norm_g": gain(ks[10], (DEPTH, D_RET)),
        "mix_w_out": nrm(ks[11], (DEPTH, D_MIX, D_MODEL), D_MIX ** -0.5),
        "ffn2_norm": gain(ks[12], (DEPTH, D_MODEL)),
        "ffn2_w_in": nrm(ks[13], (DEPTH, D_MODEL, 2 * D_FF), D_MODEL ** -0.5),
        "ffn2_w_out": nrm(ks[14], (DEPTH, D_FF, D_MODEL), D_FF ** -0.5),
        "final_norm": gain(ks[15], (D_MODEL,)),
    }

def first_block(x, ffn1_norm, ffn1_w_in, ffn1_w_out, mix_norm, mix_w_in, conv_w, conv_b,
              conv_ln_g, conv_ln_b, ret_norm_g, mix_w_out, ffn2_norm, ffn2_w_in, ffn2_w_out,
              final_norm):
    S = x.shape[1]
    pos = jnp.arange(S)
    for l in range(DEPTH):
        x = x + 0.5 * swiglu(rms_norm(x, ffn1_norm[l]), ffn1_w_in[l], ffn1_w_out[l])
        x = x + hybrid_mixer(rms_norm(x, mix_norm[l]), mix_w_in[l], conv_w[l], conv_b[l],
                             conv_ln_g[l], conv_ln_b[l], ret_norm_g[l], mix_w_out[l], pos)
        x = x + 0.5 * swiglu(rms_norm(x, ffn2_norm[l]), ffn2_w_in[l], ffn2_w_out[l])
    return rms_norm(x, final_norm)


GRID_W = 64
CTX_LEN = 256
N_HEADS = 8
Q_LORA = 384
KV_LORA = 256
QK_NOPE = 64
QK_ROPE = 32
V_HEAD = 64
ATTN_SCALE = (QK_NOPE + QK_ROPE) ** -0.5
HY_WIDTH = 512
HY_EMB = 17
HY_FILTER_HIDDEN = 64
HY_DECAY_MIN = -math.log(1e-2) / 1.5
HY_DECAY_MAX = -math.log(1e-2) / 0.3
D_FF_2 = 2816
N_EXPERTS = 8
TOP_K = 2
N_DENSE = (DEPTH + 1) // 2
N_MOE = DEPTH // 2
KV_START = Q_LORA
HY_START = KV_START + KV_LORA + QK_ROPE
GATE_START = HY_START + 3 * HY_WIDTH
IN_COLS = GATE_START + 2 * D_MODEL


def rmsnorm(x, g):
    xf = x.astype(jnp.float32)
    xf = xf * lax.rsqrt(jnp.mean(xf * xf, axis=-1, keepdims=True) + EPS)
    return xf.astype(x.dtype) * g

def adaln(cond, w, b, n_chunks):
    return jnp.split(jax.nn.silu(cond) @ w + b, n_chunks, axis=-1)

def axial_rope_tables(rows, dtype):
    n_freq = QK_ROPE // 4
    inv_freq = ROPE_BASE ** (-jnp.arange(n_freq, dtype=jnp.float32) / n_freq)
    r = jnp.repeat(jnp.arange(rows, dtype=jnp.float32), GRID_W)
    col = jnp.tile(jnp.arange(GRID_W, dtype=jnp.float32), rows)
    ang = jnp.concatenate([r[:, None] * inv_freq, col[:, None] * inv_freq], axis=-1)
    return jnp.cos(ang).astype(dtype), jnp.sin(ang).astype(dtype)

def apply_rope(v, cos, sin):
    half = QK_ROPE // 2
    a, b = v[..., :half], v[..., half:]
    return jnp.concatenate([a * cos - b * sin, b * cos + a * sin], axis=-1)

def mla_queries(p_q, q_norm_g, w_uq, rope):
    bsz, n, _ = p_q.shape
    q = (rmsnorm(p_q, q_norm_g) @ w_uq).reshape(bsz, n, N_HEADS, QK_NOPE + QK_ROPE)
    if rope is None:
        return q
    cos, sin = rope
    return jnp.concatenate([q[..., :QK_NOPE], apply_rope(q[..., QK_NOPE:], cos[:, None], sin[:, None])], axis=-1)

def mla_keys_values(p_kv, kv_norm_g, w_uk, w_uv, rope):
    bsz, n, _ = p_kv.shape
    c_kv = rmsnorm(p_kv[..., :KV_LORA], kv_norm_g)
    k_rope = p_kv[..., KV_LORA:]
    if rope is not None:
        k_rope = apply_rope(k_rope, *rope)
    k_nope = (c_kv @ w_uk).reshape(bsz, n, N_HEADS, QK_NOPE)
    v = (c_kv @ w_uv).reshape(bsz, n, N_HEADS, V_HEAD)
    k = jnp.concatenate([k_nope, jnp.broadcast_to(k_rope[:, :, None, :], (bsz, n, N_HEADS, QK_ROPE))], axis=-1)
    return k, v

def attend(q, k, v):
    s = jnp.einsum('bqhd,bkhd->bhqk', q, k).astype(jnp.float32) * ATTN_SCALE
    p = jax.nn.softmax(s, axis=-1).astype(v.dtype)
    return jnp.einsum('bhqk,bkhd->bqhd', p, v)

def attend_blocked(q, k, v):
    bsz, n, h, dk = q.shape
    qb = q.reshape(bsz, n // Q_BLOCK, Q_BLOCK, h, dk).transpose(1, 0, 2, 3, 4)
    o = lax.map(lambda qi: attend(qi, k, v), qb)
    return o.transpose(1, 0, 2, 3, 4).reshape(bsz, n, h * V_HEAD)

def hyena_filter(n, w1, b1, w2, b2, w3, freq, decay):
    f32 = jnp.float32
    w1, b1, w2, b2, w3, freq, decay = (a.astype(f32) for a in (w1, b1, w2, b2, w3, freq, decay))
    bands = (HY_EMB - 1) // 2
    t = jnp.linspace(0.0, 1.0, n, dtype=f32)[:, None]
    phase = (2.0 * math.pi / n) * jnp.arange(n, dtype=f32)[:, None] * jnp.linspace(1e-4, bands - 1, bands, dtype=f32)
    z = jnp.concatenate([t, jnp.cos(phase), -jnp.sin(phase)], axis=-1)
    h = jnp.sin(freq * (z @ w1 + b1))
    h = jnp.sin(freq * (h @ w2 + b2))
    h = (h @ w3).reshape(n, 2, HY_WIDTH) * jnp.exp(-t[:, :, None] * jnp.abs(decay))
    k = jnp.concatenate([h[:, 0], jnp.zeros((1, HY_WIDTH), f32), h[:0:-1, 1]], axis=0)
    return k / jnp.sum(jnp.abs(k), axis=0, keepdims=True)

def hyena(p, short_w, short_b, w1, b1, w2, b2, w3, freq, decay, bias):
    n = p.shape[1]
    pp = jnp.pad(p, ((0, 0), (1, 1), (0, 0)))
    u = pp[:, :-2] * short_w[0] + pp[:, 1:-1] * short_w[1] + pp[:, 2:] * short_w[2] + short_b
    v, x1, x0 = jnp.split(u, 3, axis=-1)
    z = v * x1
    k = hyena_filter(n, w1, b1, w2, b2, w3, freq, decay)
    zf = z.astype(jnp.float32)
    y = jnp.fft.irfft(jnp.fft.rfft(zf, n=2 * n, axis=1) * jnp.fft.rfft(k, axis=0)[None], n=2 * n, axis=1)[:, :n]
    y = (y + zf * bias.astype(jnp.float32)).astype(z.dtype)
    return y * x0

def token_mixer(p, k_all, v_all, rope, q_norm_g, w_uq, hy, w_br_attn, w_br_hy, w_out):
    bsz, n, _ = p.shape
    q = mla_queries(p[..., :Q_LORA], q_norm_g, w_uq, rope)
    if rope is None:
        o_attn = attend(q, k_all, v_all).reshape(bsz, n, N_HEADS * V_HEAD)
    else:
        o_attn = attend_blocked(q, k_all, v_all)
    o_hy = hyena(p[..., HY_START:GATE_START], *hy)
    g_attn, g_hy = jnp.split(jax.nn.sigmoid(p[..., GATE_START:]), 2, axis=-1)
    merged = g_attn * (o_attn @ w_br_attn) + g_hy * (o_hy @ w_br_hy)
    return merged @ w_out

def swiglu_2(h, w_gate, w_up, w_down):
    return (jax.nn.silu(h @ w_gate) * (h @ w_up)) @ w_down

def moe_swiglu(h, router, w_gate, w_up, w_down):
    bsz, n, d = h.shape
    t = h.reshape(-1, d)
    logits = (t @ router).astype(jnp.float32)
    top_val, top_idx = lax.top_k(logits, TOP_K)
    top_w = jax.nn.softmax(top_val, axis=-1)
    combine = jnp.sum(jax.nn.one_hot(top_idx, N_EXPERTS, dtype=jnp.float32) * top_w[..., None], axis=1).astype(h.dtype)
    out = jnp.zeros_like(t)
    for e in range(N_EXPERTS):
        out = out + combine[:, e:e + 1] * swiglu_2(t, w_gate[e], w_up[e], w_down[e])
    return out.reshape(bsz, n, d)

def channel_mixer(h, layer, ffn_w_gate, ffn_w_up, ffn_w_down, moe_router, moe_w_gate, moe_w_up, moe_w_down):
    i = layer // 2
    if layer % 2 == 0:
        return swiglu_2(h, ffn_w_gate[i], ffn_w_up[i], ffn_w_down[i])
    return moe_swiglu(h, moe_router[i], moe_w_gate[i], moe_w_up[i], moe_w_down[i])

def second_inputs(seed: int = 0) -> dict:
    key = jax.random.key(seed)
    ks = iter(jax.random.split(key, 48))
    f32 = jnp.float32
    D, L = D_MODEL, DEPTH

    def nrm(shape, fan_in, gain=1.0):
        return jax.random.normal(next(ks), shape, f32) * (gain * fan_in ** -0.5)

    def gain_vec(shape):
        return 1.0 + 0.02 * jax.random.normal(next(ks), shape, f32)

    def small(shape, scale):
        return scale * jax.random.normal(next(ks), shape, f32)

    return {
        'x': jax.random.normal(next(ks), (BATCH, SEQ, D), f32),
        'c': jax.random.normal(next(ks), (BATCH, D), f32),
        'ctx': jax.random.normal(next(ks), (BATCH, CTX_LEN, D), f32),
        'c_ctx': jax.random.normal(next(ks), (D,), f32),
        'w_mod': nrm((L, D, 6 * D), D, 0.5),
        'b_mod': small((L, 6 * D), 0.02),
        'norm1_g': gain_vec((L, D)),
        'norm2_g': gain_vec((L, D)),
        'w_in': nrm((L, D, IN_COLS), D),
        'q_norm_g': gain_vec((L, Q_LORA)),
        'kv_norm_g': gain_vec((L, KV_LORA)),
        'w_uq': nrm((L, Q_LORA, N_HEADS * (QK_NOPE + QK_ROPE)), Q_LORA),
        'w_uk': nrm((L, KV_LORA, N_HEADS * QK_NOPE), KV_LORA),
        'w_uv': nrm((L, KV_LORA, N_HEADS * V_HEAD), KV_LORA),
        'hy_short_w': nrm((L, 3, 3 * HY_WIDTH), 3),
        'hy_short_b': small((L, 3 * HY_WIDTH), 0.02),
        'hy_w1': nrm((L, HY_EMB, HY_FILTER_HIDDEN), HY_EMB),
        'hy_b1': small((L, HY_FILTER_HIDDEN), 0.1),
        'hy_w2': nrm((L, HY_FILTER_HIDDEN, HY_FILTER_HIDDEN), HY_FILTER_HIDDEN),
        'hy_b2': small((L, HY_FILTER_HIDDEN), 0.1),
        'hy_w3': nrm((L, HY_FILTER_HIDDEN, 2 * HY_WIDTH), HY_FILTER_HIDDEN),
        'hy_freq': gain_vec((L, HY_FILTER_HIDDEN)),
        'hy_decay': jax.random.uniform(next(ks), (L, 2, HY_WIDTH), f32, minval=HY_DECAY_MIN, maxval=HY_DECAY_MAX),
        'hy_bias': jax.random.normal(next(ks), (L, HY_WIDTH), f32),
        'w_br_attn': nrm((L, N_HEADS * V_HEAD, D), N_HEADS * V_HEAD),
        'w_br_hy': nrm((L, HY_WIDTH, D), HY_WIDTH),
        'w_out': nrm((L, D, D), D),
        'ffn_w_gate': nrm((N_DENSE, D, D_FF_2), D),
        'ffn_w_up': nrm((N_DENSE, D, D_FF_2), D),
        'ffn_w_down': nrm((N_DENSE, D_FF_2, D), D_FF_2),
        'moe_router': nrm((N_MOE, D, N_EXPERTS), D),
        'moe_w_gate': nrm((N_MOE, N_EXPERTS, D, D_FF_2), D),
        'moe_w_up': nrm((N_MOE, N_EXPERTS, D, D_FF_2), D),
        'moe_w_down': nrm((N_MOE, N_EXPERTS, D_FF_2, D), D_FF_2),
        'final_g': gain_vec((D,)),
    }

def second_block(x, c, ctx, c_ctx, w_mod, b_mod, norm1_g, norm2_g, w_in, q_norm_g, kv_norm_g, w_uq, w_uk, w_uv,
              hy_short_w, hy_short_b, hy_w1, hy_b1, hy_w2, hy_b2, hy_w3, hy_freq, hy_decay, hy_bias,
              w_br_attn, w_br_hy, w_out, ffn_w_gate, ffn_w_up, ffn_w_down,
              moe_router, moe_w_gate, moe_w_up, moe_w_down, final_g):
    rows = x.shape[1] // GRID_W
    rope = axial_rope_tables(rows, x.dtype)
    for layer in range(DEPTH):
        last = layer == DEPTH - 1
        sh1, sc1, g1, sh2, sc2, g2 = (m[:, None, :] for m in adaln(c, w_mod[layer], b_mod[layer], 6))
        hy = (hy_short_w[layer], hy_short_b[layer], hy_w1[layer], hy_b1[layer], hy_w2[layer], hy_b2[layer],
              hy_w3[layer], hy_freq[layer], hy_decay[layer], hy_bias[layer])

        h_lat = rmsnorm(x, norm1_g[layer]) * (1 + sc1) + sh1
        p_lat = h_lat @ w_in[layer]
        k_lat, v_lat = mla_keys_values(p_lat[..., KV_START:HY_START], kv_norm_g[layer], w_uk[layer], w_uv[layer], rope)

        if last:
            csh1, csc1 = adaln(c_ctx, w_mod[layer][:, :2 * D_MODEL], b_mod[layer][:2 * D_MODEL], 2)
            h_ctx = rmsnorm(ctx, norm1_g[layer]) * (1 + csc1) + csh1
            p_ctx_kv = h_ctx @ w_in[layer][:, KV_START:HY_START]
            k_ctx, v_ctx = mla_keys_values(p_ctx_kv, kv_norm_g[layer], w_uk[layer], w_uv[layer], None)
        else:
            csh1, csc1, cg1, csh2, csc2, cg2 = adaln(c_ctx, w_mod[layer], b_mod[layer], 6)
            h_ctx = rmsnorm(ctx, norm1_g[layer]) * (1 + csc1) + csh1
            p_ctx = h_ctx @ w_in[layer]
            k_ctx, v_ctx = mla_keys_values(p_ctx[..., KV_START:HY_START], kv_norm_g[layer], w_uk[layer], w_uv[layer], None)
            mix_ctx = token_mixer(p_ctx, k_ctx, v_ctx, None, q_norm_g[layer], w_uq[layer], hy,
                                  w_br_attn[layer], w_br_hy[layer], w_out[layer])

        k_all = jnp.concatenate([k_ctx, k_lat], axis=1)
        v_all = jnp.concatenate([v_ctx, v_lat], axis=1)
        mix_lat = token_mixer(p_lat, k_all, v_all, rope, q_norm_g[layer], w_uq[layer], hy,
                              w_br_attn[layer], w_br_hy[layer], w_out[layer])
        x = x + g1 * mix_lat
        x = x + g2 * channel_mixer(rmsnorm(x, norm2_g[layer]) * (1 + sc2) + sh2, layer,
                                   ffn_w_gate, ffn_w_up, ffn_w_down, moe_router, moe_w_gate, moe_w_up, moe_w_down)
        if not last:
            ctx = ctx + cg1 * mix_ctx
            ctx = ctx + cg2 * channel_mixer(rmsnorm(ctx, norm2_g[layer]) * (1 + csc2) + csh2, layer,
                                            ffn_w_gate, ffn_w_up, ffn_w_down, moe_router, moe_w_gate, moe_w_up, moe_w_down)
    return rmsnorm(x, final_g)


def setup_inputs(seed=0):
    out = dict(first_inputs(seed))
    for name, value in second_inputs(seed + 1).items():
        if name != "x":
            out[name + "_2"] = value
    return out


def reference(
    x, ffn1_norm, ffn1_w_in, ffn1_w_out, mix_norm, mix_w_in, conv_w, conv_b, conv_ln_g,
    conv_ln_b, ret_norm_g, mix_w_out, ffn2_norm, ffn2_w_in, ffn2_w_out, final_norm, c_2, ctx_2,
    c_ctx_2, w_mod_2, b_mod_2, norm1_g_2, norm2_g_2, w_in_2, q_norm_g_2, kv_norm_g_2, w_uq_2,
    w_uk_2, w_uv_2, hy_short_w_2, hy_short_b_2, hy_w1_2, hy_b1_2, hy_w2_2, hy_b2_2, hy_w3_2,
    hy_freq_2, hy_decay_2, hy_bias_2, w_br_attn_2, w_br_hy_2, w_out_2, ffn_w_gate_2, ffn_w_up_2,
    ffn_w_down_2, moe_router_2, moe_w_gate_2, moe_w_up_2, moe_w_down_2, final_g_2,
):
    x = first_block(
        x, ffn1_norm, ffn1_w_in, ffn1_w_out, mix_norm, mix_w_in, conv_w, conv_b, conv_ln_g,
        conv_ln_b, ret_norm_g, mix_w_out, ffn2_norm, ffn2_w_in, ffn2_w_out, final_norm,
    )
    return second_block(
        x, c_2, ctx_2, c_ctx_2, w_mod_2, b_mod_2, norm1_g_2, norm2_g_2, w_in_2, q_norm_g_2,
        kv_norm_g_2, w_uq_2, w_uk_2, w_uv_2, hy_short_w_2, hy_short_b_2, hy_w1_2, hy_b1_2,
        hy_w2_2, hy_b2_2, hy_w3_2, hy_freq_2, hy_decay_2, hy_bias_2, w_br_attn_2, w_br_hy_2,
        w_out_2, ffn_w_gate_2, ffn_w_up_2, ffn_w_down_2, moe_router_2, moe_w_gate_2, moe_w_up_2,
        moe_w_down_2, final_g_2,
    )


_drawn_inputs = setup_inputs


def setup_inputs(seed=0):
    import zlib

    import numpy as np

    out = dict(_drawn_inputs(seed))
    spreads = {}
    factors = {'ffn1_norm': 2.791,
     'conv_ln_g': 4.416,
     'conv_ln_b': 5.982,
     'ret_norm_g': 5.092,
     'ffn2_norm': 4.08,
     'ctx_2': 3.856,
     'norm1_g_2': 3.638,
     'norm2_g_2': 4.852,
     'q_norm_g_2': 8.0,
     'kv_norm_g_2': 8.0,
     'w_uk_2': 2.801,
     'hy_short_b_2': 4.221,
     'hy_b1_2': 8.0,
     'hy_b2_2': 5.566,
     'hy_freq_2': 8.0,
     'hy_decay_2': 4.145,
     'final_g_2': 2.843}
    for name, (base, spread) in spreads.items():
        noise = np.random.default_rng([zlib.crc32(name.encode()), seed]).standard_normal(out[name].shape)
        drawn = base * np.exp(spread * noise) if base else spread * noise
        out[name] = __import__('jax').numpy.asarray(drawn.astype(out[name].dtype))
    for name, factor in factors.items():
        out[name] = (out[name] * factor).astype(out[name].dtype)
    return out
```

```python
from contextlib import ExitStack
import math

import concourse.bass as bass
from concourse import mybir
import numpy as np

F32 = mybir.dt.float32
F32R = mybir.dt.float32r
ALU = mybir.AluOpType
ACT = mybir.ActivationFunctionType
AX = mybir.AxisListType

T = 256
D = 1024
KT = D // 128
FF = 2816
NF = FF // 128
HALF = T // 2
EPS = 1e-6
CONV_W = 31
IN2 = 4256
HY0 = 672
GATE0 = 2208
NE = 8

RAW = 11
SPLIT = 6
FFU = 3 * NF
OFF = FFU

SCALE = (64 + 32) ** -0.5
TOP_K = 2
ROUND = 1.5 * 2.0 ** 23
TWO_PI_HI = 6.28125
TWO_PI_LO = 2 * math.pi - TWO_PI_HI
PI_BELOW = 3.1415925

PER = {
    ("pe", "layers"): {"act_to_pe": 31, "dve_to_pe": 59},
    ("pe", "experts"): {"dve_to_pe": 23},
    ("act", "layers"): {"pe_to_act": 7, "dve_to_act": 74, "act_done": 4},
    ("act", "experts"): {"dve_to_act": 22},
    ("dve", "layers"): {"pe_to_dve": 4, "act_to_dve": 120, "dve_done": 45},
    ("dve", "experts"): {"act_to_dve": 44, "dve_done": 23},
}


def ffn_order():
    out = []
    for f in range(NF):
        out += [("gate", f), ("up", f)]
        if f >= 1:
            out.append(("down", f - 1))
    return out + [("down", NF - 1)]


FFN = ffn_order()
FFN_AT = {x: n for n, x in enumerate(FFN)}


class Heard:

    def __init__(self, name, sems):
        self.name = name
        self.seen = {k: 0 for k in sems}
        self.base = {k: 0 for k in sems}

    def next(self, k):
        self.seen[k] += 1
        return self.base[k] + self.seen[k]

    def enter(self, loop, reg):
        per = PER[(self.name, loop)]
        self.keep = (dict(self.seen), dict(self.base))
        for k in self.seen:
            if per.get(k, 0):
                self.base[k] = self.base[k] + self.seen[k] + reg * per[k]
                self.seen[k] = 0
        self.start = dict(self.seen)

    def leave(self, loop, trips):
        per = PER[(self.name, loop)]
        seen, base = self.keep
        got = {k: self.seen[k] - self.start[k] for k in seen if self.seen[k] != self.start[k]}
        assert got == {k: v for k, v in per.items() if v}, (self.name, loop, got)
        for k in seen:
            self.seen[k] = seen[k] + trips * per.get(k, 0)
            self.base[k] = base[k]


def program(nc, A, out):
    with ExitStack() as ctx:
        def sb(name, shape, dt=F32):
            return ctx.enter_context(nc.sbuf_tensor(name, shape, dt))

        def sem(name):
            return ctx.enter_context(nc.semaphore(name))

        raw = sb("raw", [128, RAW, 1024])
        split_at = nc.sbuf_base
        whi = sb("whi", [128, SPLIT, 1024], F32R)
        wlo = sb("wlo", [128, SPLIT, 1024], F32R)
        S = nc.alloc_sbuf_tensor_at("scratch", [128, 2 * SPLIT * 1024], F32, offset=split_at)
        X = sb("X", [128, KT, T])
        C = sb("C", [128, KT, T])
        Hhi = sb("Hhi", [128, KT, T], F32R)
        Hlo = sb("Hlo", [128, KT, T], F32R)
        TT = sb("TT", [128, KT, T])
        Ghi = sb("Ghi", [128, KT, T], F32R)
        Glo = sb("Glo", [128, KT, T], F32R)
        m_at = nc.sbuf_base
        M = sb("M", [128, 42 * 256])
        sg = nc.alloc_sbuf_tensor_at("sg", [128, 2, T], F32, offset=m_at)
        hd = nc.alloc_sbuf_tensor_at("hd", [128, 2, T], F32, offset=m_at + 2048)
        hhi = nc.alloc_sbuf_tensor_at("hhi", [128, 2, T], F32R, offset=m_at + 4096)
        hlo = nc.alloc_sbuf_tensor_at("hlo", [128, 2, T], F32R, offset=m_at + 6144)
        comb = nc.alloc_sbuf_tensor_at("comb", [128, NE, T], F32, offset=m_at + 8192)
        route = nc.alloc_sbuf_tensor_at("route", [128, 6, 128], F32, offset=m_at + 16384)
        ident = sb("ident", [128, 128])
        ones = sb("ones", [128, 128])
        tri = sb("tri", [128, 128])
        blk = sb("blk", [128, 128])
        perm64 = sb("perm64", [128, 128])
        perm96 = sb("perm96", [96, 96])
        selk = sb("selk", [128, 2, 96])
        mask = sb("mask", [128, 384])
        mcos = sb("mcos", [96, T])
        msin = sb("msin", [96, T])
        rows = S[:, 0:640].rearrange("p (a b) -> p a b", b=128)
        PV = sb("PV", [128, 5, 128])
        PL = sb("PL", [128, 96])
        CS = sb("CS", [128, KT, 2])
        MOD = sb("MOD", [128, 2, 48, 2])
        GS = sb("GS", [128, 2, 2, 2, KT])
        R = sb("R", [128, T])
        rt = sb("rt", [128, KT, NE])
        earlier = sb("earlier", [128, NE, NE])
        small = sb("small", [128, 64])
        epsc, onec, zeroc, halfc = (small[:, 40 + i:41 + i] for i in range(4))

        def m(a, n):
            return M[:, a * 256:(a + n) * 256].rearrange("p (n t) -> p n t", t=T)

        CA, CB = m(0, 2), m(2, 2)
        QK1 = m(4, 8)
        V1 = M[:, 12 * 256:16 * 256].rearrange("p (a n) -> p a n", a=2)
        QKR = m(16, 4)
        VR = M[:, 20 * 256:22 * 256].rearrange("p (a n) -> p a n", a=2)
        GR = m(22, 2)
        rcos = M[:, 24 * 256:25 * 256]
        rsin = M[:, 25 * 256:26 * 256]
        DR = M[:, 26 * 256:32 * 256].rearrange("p (h n) -> p h n", h=4)
        VP = M[:, 32 * 256:32 * 256 + 2 * 288].rearrange("p (i n) -> p i n", i=2)
        CY = m(36, 2)
        U = m(0, 12)
        PQ = m(12, 6)
        KTt = M[0:96, 18 * 256:34 * 256].rearrange("p (h n) -> p h n", h=8)
        V2 = M[:, 34 * 256:42 * 256].rearrange("p (a n) -> p a n", a=4)

        ACC = ctx.enter_context(nc.psum_tensor("ACC", [128, KT, T], F32))
        W = ctx.enter_context(nc.psum_tensor("W", [128, 4, 512], F32))

        hs = {n: sem(n) for n in ("pe_to_act", "pe_to_dve", "act_to_pe", "act_to_dve", "dve_to_pe",
                                  "dve_to_act", "act_done", "dve_done", "dve_to_pool", "act_to_pool")}
        pe_to_act, pe_to_dve, act_to_pe, act_to_dve, dve_to_pe, dve_to_act, act_done, dve_done = (
            hs[n] for n in ("pe_to_act", "pe_to_dve", "act_to_pe", "act_to_dve", "dve_to_pe", "dve_to_act",
                            "act_done", "dve_done"))
        dve_to_pool, act_to_pool = hs["dve_to_pool"], hs["act_to_pool"]
        landed = [sem(f"landed{s}") for s in range(RAW)]
        weight_high = sem("weight_high")
        weight_split = sem("weight_split")
        weight_used = sem("weight_used")
        plain_used = sem("plain_used")
        consts_in = sem("consts_in")
        table_in = sem("table_in")
        stored = sem("stored")

        block = ctx.enter_context(nc.Block())

        def cols(w, n0, n, kt=KT):
            return (w[0:kt * 128, n0:n0 + n].rearrange("(k p) n -> p k n", p=128), kt, n)

        def ffn_units(wg, wu, u0, wd):
            us = []
            for kind, f in FFN:
                if kind == "down":
                    us.append((wd[f * 128:(f + 1) * 128, :].rearrange("p (k n) -> p k n", k=KT), KT, 128))
                else:
                    us.append(cols(wg if kind == "gate" else wu, (u0 if kind == "up" else 0) + f * 128, 128))
            return us

        def lay(w, l, n=1):
            if isinstance(l, int):
                return w[l]
            return w[bass.ds(l, 1)].rearrange("a k n -> (a k) n")

        KV_UNITS = [384, 512, 544]

        def in2_units(l, full):
            w = A["w_in_2"][l]
            at = ([0, 128, 256] if full else []) + KV_UNITS + ([HY0 + 128 * i for i in range(12)] if full else [])
            return [cols(w, a, 128) for a in at]

        def qkv_units(l, full):
            us = [cols(A["w_uq_2"][l], h * 96, 96, 3) for h in range(8)] if full else []
            us += [cols(A["w_uk_2"][l], j * 128, 128, 2) for j in range(4)]
            return us + [cols(A["w_uv_2"][l], j * 128, 128, 2) for j in range(4)]

        def merge_units(l):
            us = []
            for n in range(KT):
                us += [cols(A["w_in_2"][l], GATE0 + n * 128, 128), cols(A["w_in_2"][l], GATE0 + D + n * 128, 128),
                       cols(A["w_br_attn_2"][l], n * 128, 128, 4), cols(A["w_br_hy_2"][l], n * 128, 128, 4)]
            return us

        IN1 = 24
        LU = 2 * FFU + IN1 + KT
        MODU = 2 * 48

        class Place:

            def __init__(self, u, land):
                self.u, self.land = u, land

            def after(self, n, split=True):
                return Place(self.u + n if split else self.u, [x + len(range(s, n, RAW)) for s, x in enumerate(self.land)])

        first = Place(0, [0] * RAW)
        layers = first.after(MODU, split=False)
        PHASES1 = (("ffn1", FFU), ("in", IN1), ("out", KT), ("ffn2", FFU))
        one = Place(0, [0] * RAW)
        for _, n in PHASES1:
            one = one.after(n)
        assert one.u == LU

        def places1(l):
            p = Place(layers.u + l * one.u, [x + l * y for x, y in zip(layers.land, one.land)])
            got = {}
            for name, n in PHASES1:
                got[name] = p
                p = p.after(n)
            return got

        MIXES = (("c0", 0, True), ("x0", 0, True), ("c1", 1, False), ("x1", 1, True))
        places2, sizes2 = {}, {}
        at = Place(layers.u + 2 * one.u, [x + 2 * y for x, y in zip(layers.land, one.land)])
        for inst, l, full in MIXES:
            phases = [("ffx", FFU), ("ffc", FFU)] if inst == "c1" else []
            phases += [(inst + "in", 18 if full else 3), (inst + "qkv", 16 if full else 8)]
            phases += [(inst + "merge", 32), (inst + "out", KT)] if full else []
            for name, n in phases:
                places2[name], sizes2[name] = at, n
                at = at.after(n)
        moe_at = at

        def place_moe(e):
            per = first.after(FFU)
            return Place(moe_at.u + e * FFU, [x + e * y for x, y in zip(moe_at.land, per.land)])

        @block.sync
        def _(sp):
            def stream(units, p, before):
                for n, (src, kt, nn) in enumerate(units):
                    s = n % RAW
                    if n >= RAW:
                        sp.wait_ge(weight_split, OFF + p.u + n - RAW + 1)
                    else:
                        j = (before - 1) - ((before - 1 - s) % RAW)
                        sp.wait_ge(weight_split, OFF + p.u - before + max(j, 0) + 1)
                    sp.dma_start(raw[:, s, 0:kt * nn].rearrange("p (k n) -> p k n", k=kt), src).then_inc(landed[s], 16)

            for n in range(MODU):
                src, kt, nn = cols(A["w_mod_2"][n // 48], n % 48 * 128, 128)
                if n >= RAW:
                    sp.wait_ge(plain_used, n - RAW + 1)
                sp.dma_start(raw[:, n % RAW, :].rearrange("p (k n) -> p k n", k=kt), src).then_inc(landed[n % RAW], 16)
            sp.wait_ge(plain_used, MODU)
            with sp.Fori(0, 2) as l:
                p = places1(l)
                w1, w2 = lay(A["ffn1_w_in"], l), lay(A["ffn1_w_out"], l)
                stream(ffn_units(w1, w1, FF, w2), p["ffn1"], FFU)
                w1, w2 = lay(A["mix_w_in"], l), lay(A["mix_w_out"], l)
                stream([cols(w1, n * 128, 128) for n in range(IN1)], p["in"], FFU)
                stream([cols(w2, n * 128, 128) for n in range(KT)], p["out"], IN1)
                w1, w2 = lay(A["ffn2_w_in"], l), lay(A["ffn2_w_out"], l)
                stream(ffn_units(w1, w1, FF, w2), p["ffn2"], KT)
            before = FFU

            def phase(name, units):
                nonlocal before
                assert sizes2[name] == len(units), name
                stream(units, places2[name], before)
                before = len(units)

            for inst, l, full in MIXES:
                if inst == "c1":
                    for nm in ("ffx", "ffc"):
                        phase(nm, ffn_units(A["ffn_w_gate_2"][0], A["ffn_w_up_2"][0], 0, A["ffn_w_down_2"][0]))
                phase(inst + "in", in2_units(l, full))
                phase(inst + "qkv", qkv_units(l, full))
                if full:
                    phase(inst + "merge", merge_units(l))
                    phase(inst + "out", [cols(A["w_out_2"][l], n * 128, 128) for n in range(KT)])
            sp.wait_ge(weight_split, OFF + moe_at.u)
            with sp.Fori(0, NE) as e:
                wg, wu, wd = (lay(A[k].rearrange("o e k n -> (o e) k n"), e)
                              for k in ("moe_w_gate_2", "moe_w_up_2", "moe_w_down_2"))
                stream(ffn_units(wg, wu, 0, wd), place_moe(e), FFU)

        NT = 10
        TOKENS = 1024
        CONSTS = ((ident[:, :], "k_ident"), (tri[:, :], "k_tri"), (blk[:, :], "k_blk"), (perm64[:, :], "k_perm64"),
                  (perm96[:, :], "k_perm96"), (selk[:, :, :], "k_selk"), (mask[:, :], "k_mask"), (mcos[:, :], "k_mcos"),
                  (msin[:, :], "k_msin"), (M[:, 24 * 256:26 * 256], "k_ret"), (M[:, 26 * 256:32 * 256], "k_decay"),
                  (earlier[:, :, :], "k_earlier"))
        N_CONST = len(CONSTS) + 3 + 2 * 9 + 12 + 4 + 2

        @block.gpsimd
        def _(pool):
            heard = Heard("pool", hs)
            n_const = 0

            def const(dst, src):
                nonlocal n_const
                pool.dma_start(dst, src).then_inc(consts_in, 16)
                n_const += 1

            for dst, name in CONSTS:
                const(dst, A[name])
            const(rt[:, :, :], A["moe_router_2"][0].rearrange("(k p) e -> p k e", p=128))
            for i, name in enumerate(("x", "ctx_2")):
                const(S[:, TOKENS + i * 2048:TOKENS + (i + 1) * 2048].rearrange("p (a d) -> p a d", a=2),
                      A[name][0].rearrange("(a p) d -> p a d", p=128))

            def row(t, r0, v):
                const(rows[r0:r0 + v.shape[0], t, :], v)
                return r0 + v.shape[0]

            def vec(v):
                return v.rearrange("(a b) -> a b", b=128)

            for l in range(2):
                at = 0
                for k in ("ffn1_norm", "mix_norm", "ffn2_norm", "conv_b", "conv_ln_g", "conv_ln_b", "ret_norm_g"):
                    at = row(l, at, vec(A[k][l]))
                at = row(l, at, A["conv_w"][l].rearrange("w (a b) -> (w a) b", b=128))
                assert at == 94
                row(2, 48 * l, vec(A["b_mod_2"][l]))
            at = 0
            for k in ("norm1_g_2", "norm2_g_2", "q_norm_g_2", "kv_norm_g_2", "hy_short_b_2", "hy_bias_2"):
                for l in range(2):
                    at = row(3, at, vec(A[k][l]))
            for k in (A["final_norm"], A["final_g_2"], A["c_2"][0], A["c_ctx_2"]):
                at = row(3, at, vec(k))
            assert at == 106, at
            at = 0
            for l in range(2):
                at = row(4, at, A["hy_short_w_2"][l].rearrange("w (a b) -> (w a) b", b=128))
            assert at == 72 and n_const == N_CONST, n_const
            for inst, l, full in MIXES:
                if full:
                    pool.wait_ge(dve_to_pool, heard.next("dve_to_pool"))
                    for a, n, src in ((0, 2816, A["k_dft"]), (8960, 1024, A["hy_w3_2"][l]),
                                      (7936, 1024, A["hy_decay_2"][l].rearrange("a b -> (a b)").partition_broadcast(128)),
                                      (9984, 64, A["hy_w1_2"][l]), (10048, 64, A["hy_w2_2"][l]), (10112, 256, A["k_hyz"]),
                                      (12032, 2, A["k_negt"]),
                                      (10370, 1, A["hy_freq_2"][l].rearrange("(a b) -> a b", b=1)),
                                      (10371, 1, A["hy_b1_2"][l].rearrange("(a b) -> a b", b=1)),
                                      (10372, 1, A["hy_b2_2"][l].rearrange("(a b) -> a b", b=1))):
                        pool.dma_start(S[0:src.shape[0], a:a + n], src).then_inc(table_in, 16)
            for a in range(2):
                pool.wait_ge(act_to_pool, heard.next("act_to_pool"))
                pool.dma_start(out[0, a * 128:(a + 1) * 128, :], S[:, a * 1024:(a + 1) * 1024]).then_inc(stored, 16)
            pool.wait_ge(stored, 32)

        def bank(h):
            return W[:, h, :] if h < 4 else ACC[:, 2 * (h - 4):2 * (h - 4) + 2, :].rearrange("p a t -> p (a t)")

        SZ, SE, SN, SW = (S[:, i * 3072:(i + 1) * 3072].rearrange("p (h n) -> p h n", h=8) for i in range(4))
        fc, fsn, fs0 = (S[:, i * 512:(i + 1) * 512].rearrange("p (a f) -> p a f", a=2) for i in range(3))
        fcn = S[:, 1536:1792].rearrange("p (a f) -> p a f", a=2)
        ginv = S[:, 1792:2816].rearrange("p (f t) -> p f t", f=4)
        KF = S[:, 2816:5376].rearrange("p (f n) -> p f n", f=5)
        HH = S[:, 5888:7936].rearrange("p (a s n) -> p a s n", a=2, s=2)
        DECAY = S[:, 7936:8960]
        HSUM = S[:, 7936:8960].rearrange("p (a n) -> p a n", a=2)
        w3 = S[0:64, 8960:9984]
        ENV = S[:, 9984:12032].rearrange("p (a s n) -> p a s n", a=2, s=2)
        w1s, w2s, zs = S[0:17, 9984:10048], S[0:64, 10048:10112], S[0:17, 10112:10368]
        fq, b1c, b2c = (S[0:64, c:c + 1] for c in (10370, 10371, 10372))
        negt = S[:, 12032:12034]
        u_s, k_s, s_s = (S[0:64, c:c + 256] for c in (5888, 6144, 6400))
        ZT = S[:, 9984:11008].rearrange("p (a n) -> p a n", a=2)
        YF = S[:, 7936:9984].rearrange("p (f n) -> p f n", f=4)
        TMP = S[:, 11008:12032].rearrange("p (a n) -> p a n", a=2)
        P2 = S[:, 0:1024].rearrange("p (a n) -> p a n", a=2)
        PT2 = S[:, 1024:2048].rearrange("p (a n) -> p a n", a=2)
        ROT = S[:, 2048:2048 + 512].rearrange("p (a t) -> p a t", a=2)
        DIAG = TT[:, :, :].rearrange("p k (a t) -> p k a t", a=2)
        rn = small[:, 32:36]

        QKV = lambda full: ([(3, 96)] * 8 if full else []) + [(2, 128)] * 8
        IN2 = lambda full: [(KT, 128)] * (18 if full else 3)
        MERGE = [(KT, 128), (KT, 128), (4, 128), (4, 128)] * KT
        to_in1 = lambda n: "act"
        to_in2 = lambda full: lambda n: "act" if n < (6 if full else 3) else "dve"
        to_merge = lambda n: "act" if n % 4 < 2 else "dve"

        @block.tensor
        def _(pe):
            heard = Heard("pe", hs)
            mm = nc.tensor.matmul

            def f32(o, a, b, start=True, stop=True):
                return mm(o, a, b, start=start, stop=stop, skip_group_check=True)

            def mm3(o, wh, wl, xh, xl, start, stop, swap=False):
                for i, (a, b) in enumerate(((wh, xh), (wh, xl), (wl, xh))):
                    if swap:
                        a, b = b, a
                    last = mm(o, a, b, start=start and i == 0, stop=stop and i == 2, skip_group_check=True)
                return last

            def linear(p, units, x, to, token_major=()):
                N = len(units)
                for n, (kt, nn) in enumerate(units):
                    pe.wait_ge(weight_split, OFF + p.u + n + 1)
                    if n >= 4:
                        pe.wait_ge(hs[to(n - 4) + "_to_pe"], heard.next(to(n - 4) + "_to_pe"))
                    sl = n % SPLIT
                    xh, xl = x(n)
                    parts = [slice(0, T)] if n not in token_major else [slice(0, 128), slice(128, T)]
                    for ts in parts:
                        for k in range(kt):
                            w_h, w_l = whi[:, sl, k * nn:(k + 1) * nn], wlo[:, sl, k * nn:(k + 1) * nn]
                            o = W[0:nn, n % 4, 0:T] if len(parts) == 1 else W[:, n % 4, ts]
                            last = mm3(o, w_h, w_l, xh[:, k, ts], xl[:, k, ts], k == 0, k == kt - 1, swap=len(parts) > 1)
                    last.then_inc(weight_used, 1)
                for n in range(max(N - 4, 0), N):
                    pe.wait_ge(hs[to(n) + "_to_pe"], heard.next(to(n) + "_to_pe"))

            def norm(kt=KT):
                pe.wait_ge(act_to_pe, heard.next("act_to_pe"))
                for k in range(kt):
                    last = f32(W[:, 0, 0:T], ones[:, :], TT[:, k, :], k == 0, k == kt - 1)
                last.then_inc(pe_to_act, 1)

            def ffn(p):
                pe.wait_ge(dve_to_pe, heard.next("dve_to_pe"))
                for n, (kind, f) in enumerate(FFN):
                    pe.wait_ge(weight_split, OFF + p.u + n + 1)
                    sl = n % SPLIT
                    if kind == "down":
                        pe.wait_ge(dve_to_pe, heard.next("dve_to_pe"))
                        for d in range(KT):
                            wh, wl = whi[:, sl, d * 128:(d + 1) * 128], wlo[:, sl, d * 128:(d + 1) * 128]
                            last = mm3(ACC[:, d, :], wh, wl, hhi[:, f % 2, :], hlo[:, f % 2, :],
                                       f == 0 and d % 2 == 0, f == NF - 1)
                    else:
                        o = W[:, f % 4, 0:T] if kind == "gate" else W[:, f % 4, T:2 * T]
                        for k in range(KT):
                            last = mm3(o, whi[:, sl, k * 128:(k + 1) * 128], wlo[:, sl, k * 128:(k + 1) * 128],
                                       Hhi[:, k, :], Hlo[:, k, :], k == 0, k == KT - 1)
                    last.then_inc(weight_used, 1)

            def stick_scores(q, k):
                for h in range(8):
                    b, qh, kh = bank(h), q(h), k(h)
                    f32(b[:, 0:256], kh[:, 0:128], qh)
                    last = f32(b[:, 256:384], kh[:, 128:256], qh[:, 128:256])
                last.then_inc(pe_to_act, 1)

            def values(heads, v, w, o):
                for h in range(heads):
                    f32(o(h)[0:64, 0:256], v[:, 0, h * 64:(h + 1) * 64], w[:, h, 0:256], True, False)
                    last = f32(o(h)[0:64, 128:256], v[:, 1, h * 64:(h + 1) * 64], w[:, h, 256:384], False, True)
                last.then_inc(pe_to_act, 1)

            def mix1(p):
                pe.wait_ge(dve_to_pe, heard.next("dve_to_pe"))
                linear(p["in"], [(KT, 128)] * IN1, lambda n: (Hhi, Hlo), to_in1, token_major=(12, 13, 14, 15, 20, 21))
                side = lambda h: slice(h % 2 * 64, h % 2 * 64 + 64)
                stick_scores(lambda h: QK1[side(h), h // 2, :], lambda h: QK1[side(h), 4 + h // 2, :])
                pe.wait_ge(act_to_pe, heard.next("act_to_pe"))
                for j in range(4):
                    last = f32(W[:, j, 0:T], perm64[:, :], QKR[:, j, :])
                last.then_inc(pe_to_dve, 1)
                pe.wait_ge(dve_to_pe, heard.next("dve_to_pe"))
                for h in range(8):
                    b = bank(h)
                    f32(b[:, 0:256], tri[:, :], SN[:, h, 0:256], True, False)
                    f32(b[:, 128:256], ones[:, :], SN[:, h, 256:384], False, True)
                    last = f32(b[:, 256:384], tri[:, :], SN[:, h, 256:384])
                last.then_inc(pe_to_dve, 1)
                pe.wait_ge(dve_to_pe, heard.next("dve_to_pe"))
                values(8, V1, SW, bank)
                pe.wait_ge(act_to_pe, heard.next("act_to_pe"))
                for h in range(4):
                    q, k = QKR[side(h), h // 2, :], QKR[side(h), 2 + h // 2, :]
                    f32(bank(h)[:, 0:256], k[:, 0:128], q)
                    last = f32(bank(h)[:, 256:384], k[:, 128:256], q[:, 128:256])
                last.then_inc(pe_to_dve, 1)
                pe.wait_ge(dve_to_pe, heard.next("dve_to_pe"))
                values(4, VR, SE, lambda h: bank(4 + h))
                pe.wait_ge(act_to_pe, heard.next("act_to_pe"))
                for i in range(2):
                    f32(W[:, 0, i * T:(i + 1) * T], blk[:, :], TT[:, 6 + i, :])
                for i in range(2):
                    last = f32(W[:, 1, 0:T], ones[:, :], CY[:, i, :], i == 0, i == 1)
                last.then_inc(pe_to_dve, 1)
                pe.wait_ge(act_to_pe, heard.next("act_to_pe"))
                for i in range(2):
                    f32(W[:, 0, i * T:(i + 1) * T], blk[:, :], SE[:, i, 0:T])
                for i in range(2):
                    last = f32(W[:, 1, 0:T], ones[:, :], SE[:, 2 + i, 0:T], i == 0, i == 1)
                last.then_inc(pe_to_act, 1)
                pe.wait_ge(dve_to_pe, heard.next("dve_to_pe"))
                linear(p["out"], [(KT, 128)] * KT, lambda n: (Hhi, Hlo), lambda n: "dve")

            def attention(KN):
                nk = KN // 128
                for i in range(16 + 2):
                    if i < 16:
                        h, j = i // 2, i % 2
                        f32(W[:, i % 2, 0:KN], TT[0:96, h, j * 128:(j + 1) * 128], KTt[:, h, 0:KN]
                            ).then_inc(pe_to_dve, 1)
                    if 1 <= i <= 16:
                        pe.wait_ge(dve_to_pe, heard.next("dve_to_pe"))
                        for a in range(nk):
                            last = nc.tensor.transpose(W[:, 2 + (i - 1) % 2, a * 128:(a + 1) * 128],
                                                       P2[:, (i - 1) % 2, a * 128:(a + 1) * 128], ident[:, :])
                        last.then_inc(pe_to_act, 1)
                    if i >= 2:
                        pe.wait_ge(act_to_pe, heard.next("act_to_pe"))
                        h = (i - 2) // 2
                        for a in range(nk):
                            last = f32(ACC[0:64, 2 * (i % 2), 0:128], V2[:, a, h * 64:(h + 1) * 64],
                                       PT2[:, i % 2, a * 128:(a + 1) * 128], a == 0, a == nk - 1)
                        last.then_inc(pe_to_dve, 1)

            tables = 0

            def hyena():
                nonlocal tables
                tables += NT
                pe.wait_ge(table_in, 16 * tables)
                f32(W[0:64, 0, 0:T], w1s, zs).then_inc(pe_to_dve, 1)
                pe.wait_ge(act_to_pe, heard.next("act_to_pe"))
                f32(W[0:64, 1, 0:T], w2s, s_s).then_inc(pe_to_dve, 1)
                pe.wait_ge(act_to_pe, heard.next("act_to_pe"))
                for a in range(2):
                    for c in range(2):
                        last = f32(W[:, 2 * a + c, :], s_s[:, a * 128:(a + 1) * 128], w3[:, c * 512:(c + 1) * 512])
                last.then_inc(pe_to_dve, 1)
                pe.wait_ge(act_to_pe, heard.next("act_to_pe"))
                for c in range(4):
                    for n in range(4):
                        last = f32(W[:, 0, c:c + 1], ENV[:, n // 2, n % 2, c * 128:(c + 1) * 128], ones[:, 0:1],
                                   n == 0, n == 3)
                last.then_inc(pe_to_dve, 1)
                pe.wait_ge(dve_to_pe, heard.next("dve_to_pe"))
                for f in range(5):
                    table = (fc, fc, fs0, fs0, fcn)[f]
                    o = W[:, 1, :] if f == 4 else bank(4 + f)
                    for a in range(2):
                        last = f32(o, table[:, a, f % 2 * 128:f % 2 * 128 + 128],
                                   HSUM[:, a, :] if f in (0, 1, 4) else HH[:, a, 0, :], a == 0, a == 1)
                for i in range(4):
                    for a in range(2):
                        last = nc.tensor.transpose(W[:, 2 + a, i * 128:(i + 1) * 128], U[:, i, a * 128:(a + 1) * 128],
                                                   ident[:, :])
                last.then_inc(pe_to_act, 1)
                pe.wait_ge(act_to_pe, heard.next("act_to_pe"))
                for f in range(4):
                    for a in range(2):
                        last = f32(bank(4 + f), (fc, fsn)[f // 2][:, a, f % 2 * 128:f % 2 * 128 + 128], ZT[:, a, :],
                                   a == 0, a == 1)
                last.then_inc(pe_to_dve, 1)
                pe.wait_ge(dve_to_pe, heard.next("dve_to_pe"))
                for c in range(4):
                    for f in range(4):
                        last = f32(W[:, c, 0:T], YF[:, f, c * 128:(c + 1) * 128], ginv[:, f, :], f == 0, f == 3)
                last.then_inc(pe_to_dve, 1)

            def mix2(inst, full):
                x = inst[0] == "x"
                norm()
                pe.wait_ge(dve_to_pe, heard.next("dve_to_pe"))
                linear(places2[inst + "in"], IN2(full), lambda n: (Hhi, Hlo), to_in2(full))
                for i in range(2 if x else 1):
                    last = f32(W[0:96, 1 + i, 0:T], selk[:, i, :], PQ[:, 5, :])
                last.then_inc(pe_to_dve, 1)
                for kt in ([3] if full else []) + [2]:
                    norm(kt)
                pe.wait_ge(dve_to_pe, heard.next("dve_to_pe"))
                if full:
                    pe.wait_ge(dve_to_pe, heard.next("dve_to_pe"))
                linear(places2[inst + "qkv"], QKV(full),
                       lambda n: (Ghi, Glo) if full and n < 8 else (Ghi[:, 3:5, :], Glo[:, 3:5, :]),
                       lambda n: "act", token_major=tuple(range(12 if full else 4, 16 if full else 8)))
                if not full:
                    return
                if x:
                    for h in range(8):
                        last = f32(W[0:96, h // 2, h % 2 * T:h % 2 * T + T], perm96[:, :], TT[0:96, h, :])
                    last.then_inc(pe_to_dve, 1)
                    pe.wait_ge(dve_to_pe, heard.next("dve_to_pe"))
                attention(512 if x else 256)
                hyena()
                pe.wait_ge(dve_to_pe, heard.next("dve_to_pe"))
                linear(places2[inst + "merge"], MERGE,
                       lambda n: ((Hhi, Hlo), (Hhi, Hlo), (Ghi, Glo), (Ghi[:, 4:8, :], Glo[:, 4:8, :]))[n % 4], to_merge)
                pe.wait_ge(dve_to_pe, heard.next("dve_to_pe"))
                linear(places2[inst + "out"], [(KT, 128)] * KT, lambda n: (Hhi, Hlo), lambda n: "dve")

            pe.wait_ge(consts_in, 16 * N_CONST)
            pe.wait_ge(dve_to_pe, heard.next("dve_to_pe"))
            for k in range(KT):
                for a in range(2):
                    src = TOKENS + a * D + k * 128
                    last = nc.tensor.transpose(ACC[:, k, a * 128:(a + 1) * 128], S[:, src:src + 128], ident[:, :])
            last.then_inc(pe_to_act, 1)
            for t, n in enumerate((94, 94, 96, 106, 72)):
                last = nc.tensor.transpose(W[:, t // 4, t % 4 * 128:t % 4 * 128 + n], rows[0:n, t, :], ident[0:n, 0:n])
            last.then_inc(pe_to_dve, 1)
            pe.wait_ge(dve_to_pe, heard.next("dve_to_pe"))
            for k in range(KT):
                for a in range(2):
                    src = TOKENS + 2048 + a * D + k * 128
                    last = nc.tensor.transpose(W[:, k // 2, k % 2 * T + a * 128:k % 2 * T + a * 128 + 128],
                                               S[:, src:src + 128], ident[:, :])
            last.then_inc(pe_to_act, 1)
            pe.wait_ge(act_to_pe, heard.next("act_to_pe"))
            for n in range(MODU):
                s = n % RAW
                pe.wait_ge(landed[s], 16 * (n // RAW + 1))
                for k in range(KT):
                    last = f32(W[:, n // 48, n % 48 * 2:n % 48 * 2 + 2], raw[:, s, k * 128:(k + 1) * 128], CS[:, k, :],
                               k == 0, k == KT - 1)
                last.then_inc(plain_used, 1)
            f32(ACC[:, 0, 0:2], ones[:, :], CS[:, 0, :]).then_inc(weight_used, OFF)
            with pe.Fori(0, 2) as l:
                heard.enter("layers", l)
                p = places1(l)
                norm()
                ffn(p["ffn1"])
                norm()
                mix1(p)
                norm()
                ffn(p["ffn2"])
                heard.leave("layers", 2)
            norm()
            for inst, l, full in MIXES:
                if inst == "c1":
                    for name in ("ffx", "ffc"):
                        norm()
                        ffn(places2[name])
                mix2(inst, full)
            norm()
            pe.wait_ge(dve_to_pe, heard.next("dve_to_pe"))
            for a in range(2):
                for k in range(KT):
                    for i, h in enumerate((Hhi, Hlo)):
                        last = f32(W[:, 0, a * NE:(a + 1) * NE], h[:, k, a * 128:(a + 1) * 128].bitcast(F32), rt[:, k, :],
                                   k == 0 and i == 0, k == KT - 1 and i == 1)
            last.then_inc(pe_to_dve, 1)
            pe.wait_ge(dve_to_pe, heard.next("dve_to_pe"))
            for e in range(NE):
                for a in range(2):
                    last = f32(W[:, e // 2, e % 2 * T + a * 128:e % 2 * T + a * 128 + 128], ones[:, :], DIAG[:, e, a, :])
            last.then_inc(pe_to_act, 1)
            with pe.Fori(0, NE) as e:
                heard.enter("experts", e)
                ffn(place_moe(e))
                heard.leave("experts", NE)
            norm()
            pe.wait_ge(dve_to_pe, heard.next("dve_to_pe"))
            for a in range(2):
                for k in range(KT):
                    last = nc.tensor.transpose(W[:, 2 * a + k // 4, k % 4 * 128:k % 4 * 128 + 128],
                                               TT[:, k, a * 128:(a + 1) * 128], ident[:, :])
                last.then_inc(pe_to_act, 1)

        def splitter(eng, one_unit, units):
            at = [0]

            def upto(n):
                while at[0] < min(n, len(units)):
                    one_unit(at[0], units[at[0]])
                    at[0] += 1
            return upto

        LEAD = 4

        @block.scalar
        def _(act):
            heard = Heard("act", hs)
            A_ = nc.scalar.activation

            def link(ins):
                ins.then_inc(act_done, 1)
                act.wait_ge(act_done, heard.next("act_done"))

            def tell(name):
                A_(small[0:1, 50:51], small[0:1, 51:52], ACT.Copy)
                act.drain().then_inc(hs[name], 1)

            def split_units(p, units):
                def one_unit(n, size):
                    w, s, sl = size, n % RAW, n % SPLIT
                    act.wait_ge(landed[s], 16 * (p.land[s] + n // RAW + 1))
                    act.wait_ge(weight_used, OFF + p.u + (n - SPLIT + 1 if n >= SPLIT else 0))
                    A_(whi[:, sl, 0:w], raw[:, s, 0:w], ACT.Copy).then_inc(weight_high, 1)
                return splitter(act, one_unit, units)

            def linear(p, units, to, evac):
                upto = split_units(p, [a * b for a, b in units])
                upto(LEAD)
                for n in range(len(units)):
                    upto(n + 1 + LEAD)
                    if to(n) == "act":
                        act.wait_ge(weight_used, OFF + p.u + n + 1)
                        evac(n, W[:, n % 4, :]).then_inc(act_to_pe, 1)

            def norm(src, kt=KT, shift=None, dst=None, at=0, eps=True, needs="dve_to_act"):
                if needs:
                    act.wait_ge(hs[needs], heard.next(needs))
                A_(TT[:, 0:kt, :], src[:, 0:kt, :], ACT.Square).then_inc(act_to_pe, 1)
                act.wait_ge(pe_to_act, heard.next("pe_to_act"))
                A_(R[:, :], W[:, 0, 0:T], ACT.Sqrt, bias=epsc, scale=1.0 / (kt * 128)).then_inc(act_to_dve, 1)
                if dst is not None:
                    for k in range(kt):
                        act.wait_ge(dve_to_act, heard.next("dve_to_act"))
                        A_(dst[:, at + k, :], TT[:, k, :], ACT.Identity,
                           bias=zeroc if shift is None else shift(k)).then_inc(act_to_dve, 1)

            def ffn(p, upto=None):
                if upto is None:
                    upto = split_units(p, [1024] * FFU)
                for f in range(NF):
                    upto(3 * f + 5)
                    act.wait_ge(weight_used, OFF + p.u + FFN_AT[("up", f)] + 1)
                    A_(sg[:, f % 2, :], W[:, f % 4, 0:T], ACT.Silu).then_inc(act_to_dve, 1)
                    act.wait_ge(dve_to_act, heard.next("dve_to_act"))
                    if f >= 2:
                        act.wait_ge(weight_used, OFF + p.u + FFN_AT[("down", f - 2)] + 1)
                    A_(hhi[:, f % 2, :], hd[:, f % 2, :], ACT.Copy).then_inc(act_to_dve, 1)
                upto(FFU)

            def mix1(p):
                def evac(n, b):
                    if n < 2:
                        return A_(CA[:, n, :], b[:, 0:T], ACT.Copy)
                    if n < 4:
                        return A_(CB[:, n - 2, :], b[:, 0:T], ACT.Sigmoid)
                    if n < 12:
                        return A_(QK1[:, n - 4, :], b[:, 0:T], ACT.Copy)
                    if n < 16:
                        return A_(V1[:, :, (n - 12) * 128:(n - 11) * 128], b[:, 0:T].rearrange("p (a n) -> p a n", a=2), ACT.Copy)
                    if n < 20:
                        return A_(QKR[:, n - 16, :], b[:, 0:T], ACT.Copy)
                    if n < 22:
                        return A_(VR[:, :, (n - 20) * 128:(n - 19) * 128], b[:, 0:T].rearrange("p (a n) -> p a n", a=2), ACT.Copy)
                    return A_(GR[:, n - 22, :], b[:, 0:T], ACT.Silu)

                upto = split_units(p["in"], [1024] * IN1)
                upto(LEAD)
                for n in range(IN1):
                    upto(n + 1 + LEAD)
                    act.wait_ge(weight_used, OFF + p["in"].u + n + 1)
                    evac(n, W[:, n % 4, :]).then_inc(act_to_pe, 1)
                    if n == 3:
                        tell("act_to_dve")
                act.wait_ge(pe_to_act, heard.next("pe_to_act"))
                for h in range(8):
                    A_(SZ[:, h, :], bank(h)[:, 0:384], ACT.Copy, scale=0.125)
                tell("act_to_pe")
                tell("act_done")
                act.wait_ge(act_done, heard.next("act_done"))
                link(A_(SE[:, :, :], SZ[:, :, :], ACT.Abs))
                link(A_(SE[:, :, :], SE[:, :, :], ACT.Exp, scale=-1.0))
                A_(SE[:, :, :], SE[:, :, :], ACT.Ln, bias=onec).then_inc(act_to_dve, 1)
                act.wait_ge(dve_to_act, heard.next("dve_to_act"))
                A_(SW[:, :, :], SW[:, :, :], ACT.Exp).then_inc(act_to_dve, 1)
                act.wait_ge(pe_to_act, heard.next("pe_to_act"))
                for h in range(8):
                    A_(TT[h % 2 * 64:h % 2 * 64 + 64, 2 + h // 2, :], bank(h)[0:64, 0:T], ACT.Copy)
                tell("act_to_pe")
                act.wait_ge(pe_to_act, heard.next("pe_to_act"))
                for h in range(4):
                    A_(TT[h % 2 * 64:h % 2 * 64 + 64, 6 + h // 2, :], bank(4 + h)[0:64, 0:T], ACT.Copy)
                tell("act_to_pe")
                act.wait_ge(dve_to_act, heard.next("dve_to_act"))
                for i in range(2):
                    A_(SE[:, i, 0:T], TT[:, 6 + i, :], ACT.Square)
                    A_(SE[:, 2 + i, 0:T], CY[:, i, :], ACT.Square)
                tell("act_to_pe")
                act.wait_ge(pe_to_act, heard.next("pe_to_act"))
                A_(SN[:, 0:2, 0:T], W[:, 0, :].rearrange("p (a t) -> p a t", a=2), ACT.Sqrt, bias=epsc)
                A_(SN[:, 2, 0:T], W[:, 1, 0:T], ACT.Sqrt, bias=epsc, scale=1.0 / 256)
                tell("act_to_dve")
                act.wait_ge(dve_to_act, heard.next("dve_to_act"))
                for i in range(2):
                    A_(TT[:, i, :], CY[:, i, :], ACT.Silu, bias=PL[:, 28 + i:29 + i])
                tell("act_done")
                act.wait_ge(act_done, heard.next("act_done"))
                split_x(TT, 0, Hhi, 0, 8)
                linear(p["out"], [(KT, 128)] * KT, lambda n: "dve", None)

            def split_x(src, a, dst, b, n):
                A_(dst[:, b:b + n, :], src[:, a:a + n, :], ACT.Copy).then_inc(act_to_dve, 1)

            def attention(KN):
                for i in range(17):
                    if i < 16:
                        act.wait_ge(dve_to_act, heard.next("dve_to_act"))
                        c = i % 2 * 4
                        A_(P2[:, i % 2, 0:KN], W[:, i % 2, 0:KN], ACT.Exp, bias=small[:, c:c + 1], scale=SCALE,
                           accum_out=small[:, c + 1:c + 2]).then_inc(act_to_dve, 1)
                    if i >= 1:
                        act.wait_ge(pe_to_act, heard.next("pe_to_act"))
                        A_(PT2[:, (i - 1) % 2, 0:KN], W[:, 2 + (i - 1) % 2, 0:KN], ACT.Copy).then_inc(act_to_pe, 1)

            def hyena():
                for _ in range(2):
                    act.wait_ge(dve_to_act, heard.next("dve_to_act"))
                    A_(s_s, u_s, ACT.Sin).then_inc(act_to_pe, 1)
                act.wait_ge(dve_to_act, heard.next("dve_to_act"))
                link(A_(DECAY, DECAY, ACT.Abs))
                for a in range(2):
                    A_(ENV[:, a, :, :].rearrange("p s n -> p (s n)"), DECAY, ACT.Exp, scale=negt[:, a:a + 1])
                tell("act_to_dve")
                act.wait_ge(dve_to_act, heard.next("dve_to_act"))
                A_(ENV[:, :, :, :], HH[:, :, :, :], ACT.Abs).then_inc(act_to_pe, 1)
                act.wait_ge(pe_to_act, heard.next("pe_to_act"))
                for f in range(5):
                    A_(KF[:, f, :], W[:, 1, :] if f == 4 else bank(4 + f), ACT.Copy)
                A_(ZT[:, :, :], W[:, 2:4, :], ACT.Copy)
                tell("act_to_pe")

            def mix2(inst, full, l):
                x = inst[0] == "x"
                st = 0 if x else 1
                t0 = T if x else 0
                norm(X if x else C, shift=lambda k: MOD[:, l, k, st:st + 1], dst=Hhi)

                def evac_in(n, b):
                    return A_(PQ[:, n if full else n + 3, :], b[:, 0:T], ACT.Copy)

                linear(places2[inst + "in"], IN2(full), to_in2(full), evac_in)
                tell("act_done")
                act.wait_ge(act_done, heard.next("act_done"))
                if full:
                    norm(PQ, 3, dst=Ghi, needs=None)
                norm(PQ[:, 3:5, :], 2, dst=Ghi, at=3, needs="dve_to_act" if full else None)

                def evac_qkv(n, b):
                    if full and n < 8:
                        return A_(TT[0:96, n, :], b[0:96, 0:T], ACT.Copy)
                    n -= 8 if full else 0
                    if n < 4:
                        A_(KTt[0:64, 2 * n, t0:t0 + T], b[0:64, 0:T], ACT.Copy)
                        return A_(KTt[0:64, 2 * n + 1, t0:t0 + T], b[64:128, 0:T], ACT.Copy)
                    n -= 4
                    return A_(V2[:, t0 // 128:t0 // 128 + 2, n * 128:(n + 1) * 128],
                              b[:, 0:T].rearrange("p (a n) -> p a n", a=2), ACT.Copy)

                linear(places2[inst + "qkv"], QKV(full), lambda n: "act", evac_qkv)
                if not full:
                    return
                attention(512 if x else 256)
                hyena()
                act.wait_ge(dve_to_act, heard.next("dve_to_act"))
                split_x(PQ, 0, Ghi, 0, 4)
                split_x(U, 4, Ghi, 4, 4)

                def evac_merge(n, b):
                    j, w = n // 4, n % 4
                    return A_(PQ[:, (4, 2)[j % 2] + w, :], b[:, 0:T], ACT.Sigmoid)

                p = places2[inst + "merge"]
                upto = split_units(p, [a * b for a, b in MERGE])
                upto(LEAD)
                for n in range(len(MERGE)):
                    upto(n + 1 + LEAD)
                    if to_merge(n) == "act":
                        act.wait_ge(weight_used, OFF + p.u + n + 1)
                        evac_merge(n, W[:, n % 4, :]).then_inc(act_to_pe, 1)
                        if n % 4 == 1:
                            tell("act_to_dve")
                act.wait_ge(dve_to_act, heard.next("dve_to_act"))
                split_x(TT, 0, Hhi, 0, 8)
                linear(places2[inst + "out"], [(KT, 128)] * KT, lambda n: "dve", None)

            act.wait_ge(pe_to_act, heard.next("pe_to_act"))
            for b in range(4):
                A_(X[:, 2 * b:2 * b + 2, :], ACC[:, 2 * b:2 * b + 2, :], ACT.Copy)
            act.wait_ge(dve_to_act, heard.next("dve_to_act"))
            for i in range(2):
                A_(CS[:, :, i], PV[:, 3, 90 + 8 * i:98 + 8 * i], ACT.Silu)
            act.wait_ge(pe_to_act, heard.next("pe_to_act"))
            for b in range(4):
                A_(C[:, 2 * b:2 * b + 2, :], W[:, b, :].rearrange("p (k t) -> p k t", k=2), ACT.Copy)
            tell("act_to_pe")
            tell("act_done")
            act.wait_ge(act_done, heard.next("act_done"))
            with act.Fori(0, 2) as l:
                heard.enter("layers", l)
                p = places1(l)
                norm(X, dst=Hhi)
                ffn(p["ffn1"])
                norm(X, dst=Hhi)
                mix1(p)
                norm(X, dst=Hhi)
                ffn(p["ffn2"])
                heard.leave("layers", 2)
            norm(X)
            for inst, l, full in MIXES:
                if inst == "c1":
                    for name, st, src in (("ffx", 0, X), ("ffc", 1, C)):
                        norm(src, shift=lambda k: MOD[:, 0, 24 + k, st:st + 1], dst=Hhi)
                        ffn(places2[name])
                mix2(inst, full, l)
            norm(X, shift=lambda k: MOD[:, 1, 24 + k, 0:1], dst=Hhi)
            act.wait_ge(dve_to_act, heard.next("dve_to_act"))
            A_(route[:, 1, 0:16], route[:, 1, 0:16], ACT.Exp).then_inc(act_to_dve, 1)
            act.wait_ge(pe_to_act, heard.next("pe_to_act"))
            for b in range(4):
                A_(comb[:, 2 * b:2 * b + 2, :], W[:, b, :].rearrange("p (k t) -> p k t", k=2), ACT.Copy)
            tell("act_to_dve")
            with act.Fori(0, NE) as e:
                heard.enter("experts", e)
                ffn(place_moe(e))
                heard.leave("experts", NE)
            norm(X)
            for a in range(2):
                act.wait_ge(pe_to_act, heard.next("pe_to_act"))
                for b in range(2):
                    A_(S[:, a * 1024 + b * 512:a * 1024 + b * 512 + 512], W[:, 2 * a + b, :], ACT.Copy)
                tell("act_to_pool")

        @block.vector
        def _(dve):
            heard = Heard("dve", hs)
            V = nc.vector

            def link(ins):
                ins.then_inc(dve_done, 1)
                dve.wait_ge(dve_done, heard.next("dve_done"))

            def tell(name):
                V.memset(small[0:1, 48:49], 0.0)
                dve.drain().then_inc(hs[name], 1)

            def settle():
                tell("dve_done")
                dve.wait_ge(dve_done, heard.next("dve_done"))

            def split_units(p, units):
                def one_unit(n, w):
                    s, sl = n % RAW, n % SPLIT
                    dve.wait_ge(weight_high, p.u + n + 1)
                    V.tensor_tensor(wlo[:, sl, 0:w], raw[:, s, 0:w], whi[:, sl, 0:w].bitcast(F32), ALU.subtract
                                    ).then_inc(weight_split, 1)
                return splitter(dve, one_unit, units)

            def linear(p, units, to, evac, extra=None):
                upto = split_units(p, [a * b for a, b in units])
                upto(LEAD)
                for n in range(len(units)):
                    upto(n + 1 + LEAD)
                    if to(n) == "dve":
                        dve.wait_ge(weight_used, OFF + p.u + n + 1)
                        evac(n, W[:, n % 4, :])
                    if extra is not None:
                        extra(n)

            def norm(src, gain, kt=KT, shift=None, hi=None, lo=None, at=0, to=None, told=True):
                if told:
                    tell("dve_to_act")
                dve.wait_ge(act_to_dve, heard.next("act_to_dve"))
                link(V.reciprocal(R[:, :], R[:, :]))
                for k in range(kt):
                    ins = V.scalar_tensor_tensor((TT if to is None else to)[:, k, :], src[:, k, :], gain(k), R[:, :],
                                                 ALU.mult, ALU.mult)
                    if hi is not None:
                        ins.then_inc(dve_to_act, 1)
                if hi is None:
                    settle()
                    return
                for k in range(kt):
                    dve.wait_ge(act_to_dve, heard.next("act_to_dve"))
                    ins = V.scalar_tensor_tensor(lo[:, at + k, :], TT[:, k, :], 0.0 if shift is None else shift(k),
                                                 hi[:, at + k, :].bitcast(F32), ALU.add, ALU.subtract)
                ins.then_inc(dve_to_pe, 1)

            def ffn(p, gate, res, e=None):
                upto = split_units(p, [1024] * FFU)
                for f in range(NF):
                    upto(3 * f + 5)
                    dve.wait_ge(act_to_dve, heard.next("act_to_dve"))
                    ins = V.tensor_tensor(hd[:, f % 2, :], sg[:, f % 2, :], W[:, f % 4, T:2 * T], ALU.mult)
                    if e is not None:
                        link(ins)
                        ins = V.tensor_tensor(hd[:, f % 2, :].unsqueeze(1), hd[:, f % 2, :].unsqueeze(1),
                                              comb[:, bass.ds(e, 1), :], ALU.mult)
                    ins.then_inc(dve_to_act, 1)
                    dve.wait_ge(act_to_dve, heard.next("act_to_dve"))
                    V.tensor_tensor(hlo[:, f % 2, :], hd[:, f % 2, :], hhi[:, f % 2, :].bitcast(F32), ALU.subtract
                                    ).then_inc(dve_to_pe, 1)
                upto(FFU)
                dve.wait_ge(weight_used, OFF + p.u + FFU)
                for n in range(KT):
                    V.scalar_tensor_tensor(res[:, n, :], ACC[:, n, :], gate(n), res[:, n, :], ALU.mult, ALU.add)

            def split_lo(src, a, hi, lo, b, n):
                dve.wait_ge(act_to_dve, heard.next("act_to_dve"))
                return V.tensor_tensor(lo[:, b:b + n, :], src[:, a:a + n, :], hi[:, b:b + n, :].bitcast(F32), ALU.subtract)

            def rotate(dst, src, swapped, cos, sin, tmp):
                V.tensor_tensor(tmp[0], src, cos, ALU.mult)
                link(V.tensor_tensor(tmp[1], swapped, sin, ALU.mult))
                V.tensor_tensor(dst, tmp[0], tmp[1], ALU.add)

            def mix1(p):
                taps = []
                for j in range(CONV_W):
                    for i in range(2):
                        taps.append((j, i))

                def conv(n):
                    if n == 3:
                        dve.wait_ge(act_to_dve, heard.next("act_to_dve"))
                        link(V.tensor_tensor(VP[:, :, 30:30 + T], CA[:, :, :], CB[:, :, :], ALU.mult))
                    if n >= 4:
                        for j, i in taps[4 * (n - 4):4 * (n - 3)]:
                            w = PL[:, 32 + 2 * j + i:33 + 2 * j + i]
                            if j == 0:
                                V.tensor_scalar(CY[:, i, :], VP[:, i, 0:T], w, PL[:, 24 + i:25 + i], ALU.mult, ALU.add)
                            else:
                                V.scalar_tensor_tensor(CY[:, i, :], VP[:, i, j:j + T], w, CY[:, i, :], ALU.mult, ALU.add)
                            if i == 1:
                                settle()

                linear(p["in"], [(KT, 128)] * IN1, to_in1, None, conv)
                dve.wait_ge(pe_to_dve, heard.next("pe_to_dve"))
                for j in range(4):
                    rotate(QKR[:, j, :], QKR[:, j, :], W[:, j, 0:T], rcos, rsin, (SW[:, j, 0:T], SW[:, 4 + j, 0:T]))
                dve.wait_ge(act_to_dve, heard.next("act_to_dve"))
                link(V.scalar_tensor_tensor(SN[:, :, :], SZ[:, :, :], 0.0, SE[:, :, :], ALU.max, ALU.add))
                link(V.tensor_tensor(SZ[:, :, :], SZ[:, :, :], SN[:, :, :], ALU.subtract))
                maskb = mask[:, :].unsqueeze(1).broadcast_to([128, 8, 384])
                link(V.tensor_tensor(SN[:, :, :], SN[:, :, :], maskb, ALU.mult))
                tell("dve_to_pe")
                dve.wait_ge(pe_to_dve, heard.next("pe_to_dve"))
                for h in range(8):
                    V.tensor_tensor(SW[:, h, :], SZ[:, h, :], bank(h)[:, 0:384], ALU.subtract)
                tell("dve_to_act")
                dve.wait_ge(act_to_dve, heard.next("act_to_dve"))
                V.tensor_tensor(SW[:, :, :], SW[:, :, :], maskb, ALU.mult).then_inc(dve_to_pe, 1)
                dve.wait_ge(pe_to_dve, heard.next("pe_to_dve"))
                for h in range(4):
                    V.tensor_tensor(SE[:, h, :], bank(h)[:, 0:384], DR[:, h, :], ALU.mult)
                tell("dve_to_pe")
                dve.wait_ge(pe_to_dve, heard.next("pe_to_dve"))
                for i in range(2):
                    V.tensor_tensor(TT[:, 6 + i, :], TT[:, 6 + i, :], W[:, 0, i * T:(i + 1) * T], ALU.subtract)
                    V.scalar_tensor_tensor(CY[:, i, :], W[:, 1, 0:T], -1.0 / 256, CY[:, i, :], ALU.mult, ALU.add)
                tell("dve_to_act")
                dve.wait_ge(act_to_dve, heard.next("act_to_dve"))
                link(V.reciprocal(SN[:, 0:3, 0:T], SN[:, 0:3, 0:T]))
                for i in range(2):
                    V.scalar_tensor_tensor(CY[:, i, :], CY[:, i, :], PL[:, 26 + i:27 + i], SN[:, 2, 0:T], ALU.mult, ALU.mult)
                    V.tensor_tensor(TT[:, 6 + i, :], TT[:, 6 + i, :], SN[:, i, 0:T], ALU.mult)
                settle()
                for i in range(2):
                    V.scalar_tensor_tensor(TT[:, 6 + i, :], TT[:, 6 + i, :], PL[:, 30 + i:31 + i], GR[:, i, :],
                                           ALU.mult, ALU.mult)
                tell("dve_to_act")
                split_lo(TT, 0, Hhi, Hlo, 0, 8).then_inc(dve_to_pe, 1)

                def evac(n, b):
                    V.tensor_tensor(X[:, n, :], X[:, n, :], b[:, 0:T], ALU.add).then_inc(dve_to_pe, 1)

                linear(p["out"], [(KT, 128)] * KT, lambda n: "dve", evac)

            def attention(KN, OA):
                for i in range(18):
                    c = i % 2 * 4
                    if i < 16:
                        dve.wait_ge(pe_to_dve, heard.next("pe_to_dve"))
                        link(V.tensor_reduce(small[:, c + 2:c + 3], W[:, i % 2, 0:KN], AX.X, ALU.max))
                        V.tensor_scalar(small[:, c:c + 1], small[:, c + 2:c + 3], -SCALE, None, ALU.mult
                                        ).then_inc(dve_to_act, 1)
                    if i >= 2:
                        dve.wait_ge(pe_to_dve, heard.next("pe_to_dve"))
                        h, j = (i - 2) // 2, i % 2
                        V.tensor_copy(OA[h % 2 * 64:h % 2 * 64 + 64, h // 2, j * 128:(j + 1) * 128],
                                      ACC[0:64, 2 * (i % 2), 0:128])
                    if i < 16:
                        dve.wait_ge(act_to_dve, heard.next("act_to_dve"))
                        link(V.reciprocal(small[:, c + 3:c + 4], small[:, c + 1:c + 2]))
                        V.tensor_scalar(P2[:, i % 2, 0:KN], P2[:, i % 2, 0:KN], small[:, c + 3:c + 4], None, ALU.mult
                                        ).then_inc(dve_to_pe, 1)

            tables = 0

            def sine_argument(b, o):
                link(V.tensor_scalar(u_s, o, b, fq, ALU.add, ALU.mult))
                link(V.tensor_scalar(k_s, u_s, 1.0 / (2 * math.pi), ROUND, ALU.mult, ALU.add))
                link(V.tensor_scalar(k_s, k_s, ROUND, None, ALU.subtract))
                link(V.scalar_tensor_tensor(u_s, k_s, -TWO_PI_HI, u_s, ALU.mult, ALU.add))
                link(V.scalar_tensor_tensor(u_s, k_s, -TWO_PI_LO, u_s, ALU.mult, ALU.add))
                V.tensor_scalar(u_s, u_s, PI_BELOW, -PI_BELOW, ALU.min, ALU.max).then_inc(dve_to_act, 1)

            def hyena(l):
                nonlocal tables
                settle()
                tell("dve_to_pool")
                tables += NT
                dve.wait_ge(table_in, 16 * tables)
                dve.wait_ge(pe_to_dve, heard.next("pe_to_dve"))
                sine_argument(b1c, W[0:64, 0, 0:T])
                dve.wait_ge(pe_to_dve, heard.next("pe_to_dve"))
                sine_argument(b2c, W[0:64, 1, 0:T])
                dve.wait_ge(pe_to_dve, heard.next("pe_to_dve"))
                tell("dve_to_act")
                dve.wait_ge(act_to_dve, heard.next("act_to_dve"))
                for a in range(2):
                    for s in range(2):
                        V.tensor_tensor(HH[:, a, s, :], W[:, 2 * a + s, :], ENV[:, a, s, :], ALU.mult)
                settle()
                link(V.memset(HH[0:1, 0, 1, :], 0.0))
                tell("dve_to_act")
                dve.wait_ge(pe_to_dve, heard.next("pe_to_dve"))
                V.reciprocal(rn, W[:, 0, 0:4])
                V.tensor_tensor(HSUM[:, :, :], HH[:, :, 0, :], HH[:, :, 1, :], ALU.add)
                settle()
                V.tensor_tensor(HH[:, :, 0, :], HH[:, :, 0, :], HH[:, :, 1, :], ALU.subtract).then_inc(dve_to_pe, 1)
                dve.wait_ge(pe_to_dve, heard.next("pe_to_dve"))
                for f in range(2):
                    zr, zi = bank(4 + f), bank(6 + f)
                    kr, ki, ka = KF[:, f, :], KF[:, 2 + f, :], KF[:, 4 if f == 0 else 1, :]
                    V.tensor_tensor(YF[:, f, :], zr, kr, ALU.mult)
                    V.tensor_tensor(TMP[:, 0, :], zi, ki, ALU.mult)
                    V.tensor_tensor(YF[:, 2 + f, :], zr, ki, ALU.mult)
                    V.tensor_tensor(TMP[:, 1, :], zi, ka, ALU.mult)
                    settle()
                    V.tensor_tensor(YF[:, f, :], YF[:, f, :], TMP[:, 0, :], ALU.subtract)
                    V.tensor_tensor(YF[:, 2 + f, :], YF[:, 2 + f, :], TMP[:, 1, :], ALU.add)
                    settle()
                tell("dve_to_pe")
                for c in range(4):
                    bias = PV[:, 3, 66 + 4 * l + c:67 + 4 * l + c]
                    V.tensor_scalar(U[:, c, :], U[:, c, :], bias, None, ALU.mult)
                settle()
                dve.wait_ge(pe_to_dve, heard.next("pe_to_dve"))
                for c in range(4):
                    V.scalar_tensor_tensor(U[:, 4 + c, :], W[:, c, 0:T], rn[:, c:c + 1], U[:, c, :], ALU.mult, ALU.add)
                settle()
                V.tensor_tensor(U[:, 4:8, :], U[:, 4:8, :], U[:, 8:12, :], ALU.mult)
                settle()

            def mix2(inst, full, l):
                x = inst[0] == "x"
                st = 0 if x else 1
                t0 = T if x else 0
                res = X if x else C
                norm(res, lambda k: GS[:, l, st, 0, k:k + 1], shift=lambda k: MOD[:, l, k, st:st + 1], hi=Hhi, lo=Hlo)

                def evac_in(n, b):
                    i = n - 6
                    w = lambda j: PV[:, 4, 36 * l + 12 * j + i:36 * l + 12 * j + i + 1]
                    bias = PV[:, 3, 42 + 12 * l + i:43 + 12 * l + i]
                    link(V.tensor_scalar(U[:, i, :], b[:, 0:T], w(1), bias, ALU.mult, ALU.add))
                    link(V.scalar_tensor_tensor(U[:, i, 1:T], b[:, 0:T - 1], w(0), U[:, i, 1:T], ALU.mult, ALU.add))
                    V.scalar_tensor_tensor(U[:, i, 0:T - 1], b[:, 1:T], w(2), U[:, i, 0:T - 1], ALU.mult, ALU.add
                                           ).then_inc(dve_to_pe, 1)

                linear(places2[inst + "in"], IN2(full), to_in2(full), evac_in)
                settle()
                if full:
                    V.tensor_tensor(U[:, 0:4, :], U[:, 0:4, :], U[:, 4:8, :], ALU.mult)
                dve.wait_ge(pe_to_dve, heard.next("pe_to_dve"))
                if x:
                    link(V.tensor_tensor(ROT[64:96, 0, :], W[64:96, 1, 0:T], mcos[64:96, :], ALU.mult))
                    link(V.tensor_tensor(ROT[64:96, 1, :], W[64:96, 2, 0:T], msin[64:96, :], ALU.mult))
                    link(V.tensor_tensor(ROT[64:96, 0, :], ROT[64:96, 0, :], ROT[64:96, 1, :], ALU.add))
                else:
                    link(V.tensor_copy(ROT[64:96, 0, :], W[64:96, 1, 0:T]))
                V.tensor_copy(KTt[64:96, :, t0:t0 + T], ROT[64:96, 0, :].unsqueeze(1).broadcast_to([32, 8, T]))
                if full:
                    norm(PQ, lambda k: PV[:, 3, 32 + 3 * l + k:33 + 3 * l + k], 3, hi=Ghi, lo=Glo, told=False)
                norm(PQ[:, 3:5, :], lambda k: PV[:, 3, 38 + 2 * l + k:39 + 2 * l + k], 2, hi=Ghi, lo=Glo, at=3, told=full)
                linear(places2[inst + "qkv"], QKV(full), lambda n: "act", None)
                if not full:
                    return
                if x:
                    dve.wait_ge(pe_to_dve, heard.next("pe_to_dve"))
                    for h in range(8):
                        rotate(TT[0:96, h, :], TT[0:96, h, :], W[0:96, h // 2, h % 2 * T:h % 2 * T + T], mcos[:, :],
                               msin[:, :], (S[0:96, 4096 + 512 * h:4352 + 512 * h], S[0:96, 4352 + 512 * h:4608 + 512 * h]))
                    tell("dve_to_pe")
                attention(512 if x else 256, PQ)
                hyena(l)
                tell("dve_to_act")
                split_lo(PQ, 0, Ghi, Glo, 0, 4)
                split_lo(U, 4, Ghi, Glo, 4, 4).then_inc(dve_to_pe, 1)

                def evac_merge(n, b):
                    j = n // 4
                    if n % 4 == 2:
                        dve.wait_ge(act_to_dve, heard.next("act_to_dve"))
                        V.tensor_tensor(TT[:, j, :], PQ[:, (4, 2)[j % 2], :], b[:, 0:T], ALU.mult
                                        ).then_inc(dve_to_pe, 1)
                    else:
                        V.tensor_tensor(PQ[:, j % 2, :], PQ[:, (4, 2)[j % 2] + 1, :], b[:, 0:T], ALU.mult
                                        ).then_inc(dve_to_pe, 1)
                        settle()
                        V.tensor_tensor(TT[:, j, :], TT[:, j, :], PQ[:, j % 2, :], ALU.add)

                linear(places2[inst + "merge"], MERGE, to_merge, evac_merge)
                tell("dve_to_act")
                split_lo(TT, 0, Hhi, Hlo, 0, 8).then_inc(dve_to_pe, 1)

                def evac_out(n, b):
                    V.scalar_tensor_tensor(res[:, n, :], b[:, 0:T], MOD[:, l, 16 + n, st:st + 1], res[:, n, :],
                                           ALU.mult, ALU.add).then_inc(dve_to_pe, 1)

                linear(places2[inst + "out"], [(KT, 128)] * KT, lambda n: "dve", evac_out)

            V.memset(ones[:, :], 1.0)
            V.memset(VP[:, :, 0:30], 0.0)
            V.memset(epsc, EPS)
            V.memset(small[0:1, 51:52], 0.0)
            V.memset(onec, 1.0)
            V.memset(zeroc, 0.0)
            V.memset(halfc, 0.5).then_inc(weight_split, OFF)
            tell("dve_to_pe")
            dve.wait_ge(pe_to_dve, heard.next("pe_to_dve"))
            V.tensor_copy(PV[:, 0:2, 0:94], W[:, 0, 0:256].rearrange("p (a n) -> p a n", a=2)[:, :, 0:94])
            V.tensor_copy(PV[:, 2, 0:96], W[:, 0, 256:352])
            V.tensor_copy(PV[:, 3, 0:106], W[:, 0, 384:490])
            V.tensor_copy(PV[:, 4, 0:72], W[:, 1, 0:72])
            tell("dve_to_pe")
            tell("dve_to_act")
            settle()
            dve.wait_ge(plain_used, MODU)
            for l in range(2):
                V.tensor_tensor(MOD[:, l, :, :], W[:, l, 0:96].rearrange("p (n s) -> p n s", s=2),
                                PV[:, 2, 48 * l:48 * l + 48].unsqueeze(2).broadcast_to([128, 48, 2]), ALU.add)
            settle()
            for l in range(2):
                for st in range(2):
                    for w in range(2):
                        V.scalar_tensor_tensor(GS[:, l, st, w, :], MOD[:, l, 8 + 24 * w:16 + 24 * w, st], 1.0,
                                               PV[:, 3, 16 * w + 8 * l:16 * w + 8 * l + 8], ALU.add, ALU.mult)
            settle()
            with dve.Fori(0, 2) as l:
                heard.enter("layers", l)
                p = places1(l)
                V.tensor_copy(PL[:, 0:94].unsqueeze(1), PV[:, bass.ds(l, 1), 0:94])
                norm(X, lambda k: PL[:, k:k + 1], hi=Hhi, lo=Hlo)
                ffn(p["ffn1"], lambda n: 0.5, X)
                norm(X, lambda k: PL[:, 8 + k:9 + k], hi=Hhi, lo=Hlo)
                mix1(p)
                norm(X, lambda k: PL[:, 16 + k:17 + k], hi=Hhi, lo=Hlo)
                ffn(p["ffn2"], lambda n: 0.5, X)
                settle()
                heard.leave("layers", 2)
            norm(X, lambda k: PV[:, 3, 74 + k:75 + k], to=X)
            for inst, l, full in MIXES:
                if inst == "c1":
                    for name, st, res in (("ffx", 0, X), ("ffc", 1, C)):
                        norm(res, lambda k: GS[:, 0, st, 1, k:k + 1], shift=lambda k: MOD[:, 0, 24 + k, st:st + 1],
                             hi=Hhi, lo=Hlo)
                        ffn(places2[name], lambda n: MOD[:, 0, 40 + n, st:st + 1], res)
                        settle()
                mix2(inst, full, l)
            norm(X, lambda k: GS[:, 1, 0, 1, k:k + 1], shift=lambda k: MOD[:, 1, 24 + k, 0:1], hi=Hhi, lo=Hlo)
            dve.wait_ge(pe_to_dve, heard.next("pe_to_dve"))
            L = route[:, 0, 0:16].rearrange("p (a e) -> p a e", a=2)
            EL = route[:, 1, 0:16].rearrange("p (a e) -> p a e", a=2)
            more = route[:, 2, :].rearrange("p (a e f) -> p a e f", a=2, e=NE)
            same = route[:, 3, :].rearrange("p (a e f) -> p a e f", a=2, e=NE)
            rank = route[:, 4, 0:16].rearrange("p (a e) -> p a e", a=2)
            link(V.tensor_copy(L, W[:, 0, 0:16].rearrange("p (a e) -> p a e", a=2)))
            V.tensor_reduce(small[:, 0:2], L, AX.X, ALU.max)
            other = L.unsqueeze(2).broadcast_to([128, 2, NE, NE])
            own = L.unsqueeze(3).broadcast_to([128, 2, NE, NE])
            V.tensor_tensor(more, other, own, ALU.is_gt)
            V.tensor_tensor(same, other, own, ALU.is_equal)
            settle()
            V.tensor_tensor(EL, L, small[:, 0:2].unsqueeze(2).broadcast_to([128, 2, NE]), ALU.subtract
                            ).then_inc(dve_to_act, 1)
            link(V.tensor_tensor(same, same, earlier[:, :, :].unsqueeze(1).broadcast_to([128, 2, NE, NE]), ALU.mult))
            link(V.tensor_tensor(more, more, same, ALU.add))
            link(V.tensor_reduce(rank, more, AX.X, ALU.add))
            link(V.tensor_scalar(rank, rank, TOP_K - 0.5, None, ALU.is_lt))
            dve.wait_ge(act_to_dve, heard.next("act_to_dve"))
            link(V.tensor_tensor(EL, EL, rank, ALU.mult))
            link(V.tensor_reduce(small[:, 2:4], EL, AX.X, ALU.add))
            link(V.reciprocal(small[:, 2:4], small[:, 2:4]))
            link(V.tensor_tensor(EL, EL, small[:, 2:4].unsqueeze(2).broadcast_to([128, 2, NE]), ALU.mult))
            for e in range(NE):
                for a in range(2):
                    V.tensor_scalar(DIAG[:, e, a, :], ident[:, :], EL[:, a, e:e + 1], None, ALU.mult)
            tell("dve_to_pe")
            dve.wait_ge(act_to_dve, heard.next("act_to_dve"))
            with dve.Fori(0, NE) as e:
                heard.enter("experts", e)
                tell("dve_to_pe")
                ffn(place_moe(e), lambda n: MOD[:, 1, 40 + n, 0:1], X, e)
                settle()
                heard.leave("experts", NE)
            norm(X, lambda k: PV[:, 3, 82 + k:83 + k])
            tell("dve_to_pe")


def tables():
    f = np.float32
    i = np.arange(128)
    t = np.arange(T)
    ident = np.eye(128)
    tri = (i[:, None] > i[None, :]) * 1.0
    blk = (i[:, None] // 64 == i[None, :] // 64) / 64.0
    perm64 = np.zeros((128, 128))
    for o in range(128):
        h, r = o // 64 * 64, o % 64
        perm64[h + (r + 32) % 64, o] = 1.0
    half = np.arange(32)
    ang = t[None, :].astype(f) * (1.0 / (f(10000.0) ** (half.astype(f) / f(32)))).astype(f)[:, None]
    rc, rs = np.cos(ang.astype(np.float64)), np.sin(ang.astype(np.float64))
    ret = np.concatenate([np.tile(rc, (4, 1)), np.tile(np.concatenate([-rs, rs]), (2, 1))], axis=1)
    perm96, selk = np.zeros((96, 96)), np.zeros((128, 2, 96))
    for r in range(32):
        perm96[64 + (r + 16) % 32, 64 + r] = 1.0
        selk[96 + r, 0, 64 + r] = 1.0
        selk[96 + (r + 16) % 32, 1, 64 + r] = 1.0
    n_freq = 8
    inv = (f(10000.0) ** (-np.arange(n_freq, dtype=f) / f(n_freq))).astype(f)
    a = np.concatenate([(t // 64).astype(f)[:, None] * inv, (t % 64).astype(f)[:, None] * inv], axis=-1).T
    mc, ms = np.cos(a.astype(np.float64)), np.sin(a.astype(np.float64))
    mcos = np.concatenate([np.ones((64, T)), mc, mc])
    msin = np.concatenate([np.zeros((64, T)), -ms, ms])
    diag = (i[:, None] < i[None, :]) * 1.0
    mask = np.concatenate([diag, np.ones((128, 128)), diag], axis=1)
    log_gamma = np.log1p(-np.exp2(-5.0 - np.arange(4)))
    s = t[:, None]
    full = np.exp(log_gamma[:, None, None] * np.abs(t[None, None, :] - s)) * (s // 64 <= t[None, :] // 64) * 0.125
    decay = np.concatenate([full[:, 0:128, :], full[:, 128:, 128:]], axis=2).transpose(1, 0, 2)
    w = 2 * np.pi * np.outer(t, t) / (2 * T)
    c, sn, alt = np.cos(w), -np.sin(w), (-1.0) ** t
    sn[:, 0] = 0.0
    snn, cn = sn.copy(), c[:, 0:128].copy()
    snn[:, 0], cn[:, 0] = alt, alt
    gc = np.cos(w) * 2 / (2 * T)
    gc[0] /= 2
    gs = -np.sin(w) * 2 / (2 * T)
    gs[0] = alt / (2 * T)
    tiles = lambda v: v.reshape(-1, 128, v.shape[1]).transpose(1, 0, 2).reshape(128, -1)
    dft = np.concatenate([tiles(c), tiles(snn), tiles(sn), tiles(cn), tiles(np.concatenate([gc, gs]))], axis=1)
    tl = np.linspace(0.0, 1.0, T, dtype=f)
    ph = (f(2.0 * math.pi / T) * t.astype(f))[:, None] * np.linspace(1e-4, 7, 8, dtype=f)
    hyz = np.concatenate([tl[:, None], np.cos(ph.astype(np.float64)), -np.sin(ph.astype(np.float64))], axis=-1).T
    earlier = np.broadcast_to((np.arange(NE)[:, None] > np.arange(NE)[None, :]) * 1.0, (128, NE, NE))
    got = dict(k_ident=ident, k_tri=tri, k_blk=blk, k_perm64=perm64, k_perm96=perm96, k_selk=selk, k_mask=mask,
               k_mcos=mcos, k_msin=msin, k_ret=ret, k_decay=decay.reshape(128, -1), k_dft=dft, k_hyz=hyz,
               k_negt=-tl.reshape(2, 128).T, k_earlier=earlier)
    return {k: np.ascontiguousarray(v, dtype=f) for k, v in got.items()}


def kernel(**inputs):
    import concourse.bacc as bacc
    from concourse.bass_utils import run_bass_kernel_spmd

    nc = bacc.Bacc("TRN2", target_bir_lowering=False, num_devices=1)
    arrays, A = {}, {}
    for name, a in [*inputs.items(), *tables().items()]:
        a = np.ascontiguousarray(a)
        arrays[f"in_{name}"] = a
        A[name] = nc.dram_tensor(f"in_{name}", a.shape, mybir.dt.from_np(a.dtype), kind="ExternalInput").ap()
    out = nc.dram_tensor("out_0", (1, T, D), F32, kind="ExternalOutput").ap()
    nc.disable_value_cache = True
    program(nc, A, out)
    r = run_bass_kernel_spmd(nc, [arrays], core_ids=[0])
    return r.results[0]["out_0"]
```

```python
from contextlib import ExitStack
import math

import concourse.bass as bass
from concourse import mybir
import numpy as np

F32 = mybir.dt.float32
F32R = mybir.dt.float32r
ALU = mybir.AluOpType
ACT = mybir.ActivationFunctionType
AX = mybir.AxisListType

T = 256
D = 1024
KT = D // 128
FF = 2816
NF = FF // 128
HALF = T // 2
EPS = 1e-6
CONV_W = 31
IN2 = 4256
HY0 = 672
GATE0 = 2208
NE = 8
ITEMS = 2 * NE

RAW = 11
SPLIT = 6
FFU = 3 * NF
MODH = 24
OFF = FFU + MODH

SCALE = (64 + 32) ** -0.5
TOP_K = 2
ROUND = 1.5 * 2.0 ** 23
TWO_PI_HI = 6.28125
TWO_PI_LO = 2 * math.pi - TWO_PI_HI
PI_BELOW = 3.1415925

PER = {
    ("pe", "items"): {"act_to_pe": 3, "dve_to_pe": 16},
    ("act", "items"): {"pe_to_act": 9, "dve_to_act": 1},
    ("dve", "items"): {"pe_to_dve": 2, "act_to_dve": 13, "dve_done": 3},
    ("pe", "layers"): {"act_to_pe": 52, "dve_to_pe": 72, "dve_rows": 12},
    ("act", "layers"): {"pe_to_act": 7, "dve_to_act": 88, "act_done": 4},
    ("dve", "layers"): {"pe_to_dve": 6, "act_to_dve": 120, "dve_done": 49},
}


def ffn_order(riders=0):
    out = []
    for f in range(NF):
        out += [("gate", f), ("up", f)]
        out += [("mod", f)] if f < riders else []
        if f >= 2:
            out.append(("down", f - 2))
    return out + [("down", NF - 2)] + [("mod", f) for f in range(NF, riders)] + [("down", NF - 1)]


FFN = ffn_order()
FFN_MOD = ffn_order(MODH)
AT = {n: {x: i for i, x in enumerate(order)} for n, order in ((FFU, FFN), (FFU + MODH, FFN_MOD))}


GROUP = 512
GROUPS = [min(GROUP, FF - c) for c in range(0, FF, GROUP)]
NG = len(GROUPS)


def item_order():
    order = []
    for g in range(NG):
        order += [(kind, g, j) for kind in ("gate", "up") for j in range(GROUPS[g] // 128)]
        if g >= 1:
            order += [("down", g - 1, j) for j in range(GROUPS[g - 1] // 128)]
    return order + [("down", NG - 1, j) for j in range(GROUPS[NG - 1] // 128)]


ITEM = item_order()


class Heard:

    def __init__(self, name, sems):
        self.name = name
        self.seen = {k: 0 for k in sems}
        self.base = {k: 0 for k in sems}

    def next(self, k):
        self.seen[k] += 1
        return self.base[k] + self.seen[k]

    def enter(self, loop, reg):
        per = PER[(self.name, loop)]
        self.keep = (dict(self.seen), dict(self.base))
        for k in self.seen:
            if per.get(k, 0):
                self.base[k] = self.base[k] + self.seen[k] + reg * per[k]
                self.seen[k] = 0
        self.start = dict(self.seen)

    def leave(self, loop, trips):
        per = PER[(self.name, loop)]
        seen, base = self.keep
        got = {k: self.seen[k] - self.start[k] for k in seen if self.seen[k] != self.start[k]}
        assert got == {k: v for k, v in per.items() if v}, (self.name, loop, got)
        for k in seen:
            self.seen[k] = seen[k] + trips * per.get(k, 0)
            self.base[k] = base[k]


def program(nc, A, out):
    with ExitStack() as ctx:
        def sb(name, shape, dt=F32):
            return ctx.enter_context(nc.sbuf_tensor(name, shape, dt))

        def sem(name):
            return ctx.enter_context(nc.semaphore(name))

        raw = sb("raw", [128, RAW, 1024])
        split_at = nc.sbuf_base
        whi = sb("whi", [128, SPLIT, 1024], F32R)
        wlo = sb("wlo", [128, SPLIT, 1024], F32R)
        S = nc.alloc_sbuf_tensor_at("scratch", [128, 2 * SPLIT * 1024], F32, offset=split_at)
        X = sb("X", [128, KT, T])
        C = sb("C", [128, KT, T])
        Hhi = sb("Hhi", [128, KT, T], F32R)
        Hlo = sb("Hlo", [128, KT, T], F32R)
        TT = sb("TT", [128, KT, T])
        Ghi = sb("Ghi", [128, KT, T], F32R)
        Glo = sb("Glo", [128, KT, T], F32R)
        m_at = nc.sbuf_base
        M = sb("M", [128, 42 * 256])
        sg = nc.alloc_sbuf_tensor_at("sg", [128, 2, T], F32, offset=m_at)
        hd = nc.alloc_sbuf_tensor_at("hd", [128, 3, T], F32, offset=m_at + 38 * 1024)
        hhi = nc.alloc_sbuf_tensor_at("hhi", [128, 2, T], F32R, offset=m_at + 4096)
        hlo = nc.alloc_sbuf_tensor_at("hlo", [128, 2, T], F32R, offset=m_at + 6144)
        MR = nc.alloc_sbuf_tensor_at("MR", [128, MODH * 128], F32, offset=m_at + 8192)
        sgt = nc.alloc_sbuf_tensor_at("sgt", [128, 2, GROUP], F32, offset=m_at)
        hdt = nc.alloc_sbuf_tensor_at("hdt", [128, 2, GROUP], F32, offset=m_at + 4096)
        hgi = nc.alloc_sbuf_tensor_at("hgi", [128, 2, GROUP], F32R, offset=m_at + 28672)
        hgo = nc.alloc_sbuf_tensor_at("hgo", [128, 2, GROUP], F32R, offset=m_at + 32768)
        Yhi = nc.alloc_sbuf_tensor_at("Yhi", [128, D], F32R, offset=m_at + 8192)
        Ylo = nc.alloc_sbuf_tensor_at("Ylo", [128, D], F32R, offset=m_at + 12288)
        route = nc.alloc_sbuf_tensor_at("route", [128, 6, 256], F32, offset=m_at + 16384)
        sel = nc.alloc_sbuf_tensor_at("sel", [128, 2, 128], F32R, offset=m_at + 22528)
        selT = nc.alloc_sbuf_tensor_at("selT", [128, T], F32R, offset=m_at + 23552)
        slots = nc.alloc_sbuf_tensor_at("slots", [128, 2 * NE, 4], F32, offset=m_at + 24576)
        plan = nc.alloc_sbuf_tensor_at("plan", [128, 64], mybir.dt.int32, offset=m_at + 24832)
        now = nc.alloc_sbuf_tensor_at("now", [128, 8], F32, offset=m_at + 25088)
        kplan = sb("kplan", [128, 672])
        ident = sb("ident", [128, 128])
        ones = sb("ones", [128, 128])
        tri = sb("tri", [128, 128])
        blk = sb("blk", [128, 128])
        perm64 = sb("perm64", [128, 128])
        perm96 = sb("perm96", [96, 96])
        selk = sb("selk", [128, 2, 96])
        mask = sb("mask", [128, 384])
        mcos = sb("mcos", [96, T])
        msin = sb("msin", [96, T])
        rows = S[:, 0:640].rearrange("p (a b) -> p a b", b=128)
        PV = sb("PV", [128, 5, 128])
        PL = sb("PL", [128, 96])
        CS = sb("CS", [128, KT, 2])
        CS4 = sb("CS4", [128, KT, 4], F32R)
        BL = sb("BL", [128, 48])
        ML = sb("ML", [128, 48, 2])
        MOD = sb("MOD", [128, 2, 48, 2])
        GS = sb("GS", [128, 2, 2, 2, KT])
        R = sb("R", [128, T])
        rt = sb("rt", [128, KT, NE])
        earlier = sb("earlier", [128, NE, NE])
        small = sb("small", [128, 64])
        epsc, onec, zeroc, halfc = (small[:, 40 + i:41 + i] for i in range(4))

        def m(a, n):
            return M[:, a * 256:(a + n) * 256].rearrange("p (n t) -> p n t", t=T)

        CA, CB = m(0, 2), m(2, 2)
        QK1 = m(4, 8)
        V1 = M[:, 12 * 256:16 * 256].rearrange("p (a n) -> p a n", a=2)
        QKR = m(16, 4)
        VR = M[:, 20 * 256:22 * 256].rearrange("p (a n) -> p a n", a=2)
        GR = m(22, 2)
        rcos = M[:, 24 * 256:25 * 256]
        rsin = M[:, 25 * 256:26 * 256]
        DR = M[:, 26 * 256:32 * 256].rearrange("p (h n) -> p h n", h=4)
        VP = M[:, 32 * 256:32 * 256 + 2 * 288].rearrange("p (i n) -> p i n", i=2)
        CY = m(36, 2)
        U = m(0, 12)
        PQ = m(12, 6)
        KTt = M[0:96, 18 * 256:34 * 256].rearrange("p (h n) -> p h n", h=8)
        V2 = M[:, 34 * 256:42 * 256].rearrange("p (a n) -> p a n", a=4)

        kept = nc.dram_tensor("kept", (128, 5 * 512), F32).ap()

        ACC = ctx.enter_context(nc.psum_tensor("ACC", [128, KT, T], F32))
        W = ctx.enter_context(nc.psum_tensor("W", [128, 4, 512], F32))

        hs = {n: sem(n) for n in ("pe_to_act", "pe_to_dve", "act_to_pe", "act_to_dve", "dve_to_pe",
                                  "dve_to_act", "dve_rows", "act_done", "dve_done", "dve_to_pool", "act_to_pool")}
        dve_rows = hs["dve_rows"]
        pe_to_act, pe_to_dve, act_to_pe, act_to_dve, dve_to_pe, dve_to_act, act_done, dve_done = (
            hs[n] for n in ("pe_to_act", "pe_to_dve", "act_to_pe", "act_to_dve", "dve_to_pe", "dve_to_act",
                            "act_done", "dve_done"))
        dve_to_pool, act_to_pool = hs["dve_to_pool"], hs["act_to_pool"]
        landed = [sem(f"landed{s}") for s in range(RAW)]
        weight_high = sem("weight_high")
        weight_split = sem("weight_split")
        weight_used = sem("weight_used")
        consts_in = sem("consts_in")
        vectors_in = sem("vectors_in")
        table_in = sem("table_in")
        stored = sem("stored")
        kept_in = sem("kept_in")
        kept_out = sem("kept_out")
        plan_ready = sem("plan_ready")

        block = ctx.enter_context(nc.Block())

        def cols(w, n0, n, kt=KT):
            return (w[0:kt * 128, n0:n0 + n].rearrange("(k p) n -> p k n", p=128), kt, n)

        def ffn_units(wg, wu, u0, wd, riders=None):
            us = []
            for kind, f in (FFN if riders is None else FFN_MOD):
                if kind == "mod":
                    at = riders[1] + f // 4 * 512
                    us.append((riders[0][f % 4 * 256:(f % 4 + 1) * 256, at:at + 512].rearrange("(k p) n -> p k n", p=128),
                               2, 512))
                elif kind == "down":
                    us.append((wd[f * 128:(f + 1) * 128, :].rearrange("p (k n) -> p k n", k=KT), KT, 128))
                else:
                    us.append(cols(wg if kind == "gate" else wu, (u0 if kind == "up" else 0) + f * 128, 128))
            return us

        def item_units(wg, wu, wd):
            us = []
            for kind, g, j in ITEM:
                n = GROUPS[g]
                if kind == "down":
                    row = g * GROUP + j * 128
                    us.append((wd[row:row + 128, :].rearrange("p (k n) -> p k n", k=KT), KT, 128))
                else:
                    kt = 1024 // n
                    w = (wg if kind == "gate" else wu)[j * kt * 128:(j + 1) * kt * 128, g * GROUP:g * GROUP + n]
                    us.append((w.rearrange("(k p) n -> p k n", p=128), kt, n))
            return us

        def lay(w, l, n=1):
            if isinstance(l, int):
                return w[l]
            return w[bass.ds(l, 1)].rearrange("a k n -> (a k) n")

        KV_UNITS = [384, 512, 544]

        def in2_units(l, full):
            w = A["w_in_2"][l]
            at = ([0, 128, 256] if full else []) + KV_UNITS + ([HY0 + 128 * i for i in range(12)] if full else [])
            return [cols(w, a, 128) for a in at]

        def qkv_units(l, full):
            us = [cols(A["w_uq_2"][l], h * 96, 96, 3) for h in range(8)] if full else []
            us += [cols(A["w_uk_2"][l], j * 128, 128, 2) for j in range(4)]
            return us + [cols(A["w_uv_2"][l], j * 128, 128, 2) for j in range(4)]

        def merge_units(l):
            us = []
            for n in range(KT):
                us += [cols(A["w_in_2"][l], GATE0 + n * 128, 128), cols(A["w_in_2"][l], GATE0 + D + n * 128, 128),
                       cols(A["w_br_attn_2"][l], n * 128, 128, 4), cols(A["w_br_hy_2"][l], n * 128, 128, 4)]
            return us

        IN1 = 24
        FF1 = FFU + MODH

        class Place:

            def __init__(self, u, land):
                self.u, self.land = u, land

            def after(self, n):
                return Place(self.u + n, [x + len(range(s, n, RAW)) for s, x in enumerate(self.land)])

        first = Place(0, [0] * RAW)
        PHASES1 = (("ffn1", FF1), ("in", IN1), ("out", KT), ("ffn2", FF1))
        one = Place(0, [0] * RAW)
        for _, n in PHASES1:
            one = one.after(n)

        def places1(l):
            p = Place(l * one.u, [l * y for y in one.land])
            got = {}
            for name, n in PHASES1:
                got[name] = p
                p = p.after(n)
            return got

        MIXES = (("c0", 0, True), ("x0", 0, True), ("c1", 1, False), ("x1", 1, True))
        places2, sizes2 = {}, {}
        at = Place(2 * one.u, [2 * y for y in one.land])
        for inst, l, full in MIXES:
            phases = [("ffx", FFU), ("ffc", FFU)] if inst == "c1" else []
            phases += [(inst + "in", 18 if full else 3), (inst + "qkv", 16 if full else 8)]
            phases += [(inst + "merge", 32), (inst + "out", KT)] if full else []
            for name, n in phases:
                places2[name], sizes2[name] = at, n
                at = at.after(n)
        moe_at = at

        def place_moe(i):
            per = first.after(FFU)
            return Place(moe_at.u + i * FFU, [x + i * y for x, y in zip(moe_at.land, per.land)])

        TOKENS = 1024
        CONSTS = ((tri[:, :], "k_tri"), (blk[:, :], "k_blk"), (perm64[:, :], "k_perm64"),
                  (perm96[:, :], "k_perm96"), (selk[:, :, :], "k_selk"), (mask[:, :], "k_mask"), (mcos[:, :], "k_mcos"),
                  (msin[:, :], "k_msin"), (M[:, 24 * 256:26 * 256], "k_ret"), (M[:, 26 * 256:32 * 256], "k_decay"),
                  (earlier[:, :, :], "k_earlier"), (kplan[:, :], "k_plan"))
        vectors = []

        def row(t, r0, v):
            vectors.append((rows[r0:r0 + v.shape[0], t, :], v))
            return r0 + v.shape[0]

        def vec(v):
            return v.rearrange("(a b) -> a b", b=128)

        for l in range(2):
            at = 0
            for k in ("ffn1_norm", "mix_norm", "ffn2_norm", "conv_b", "conv_ln_g", "conv_ln_b", "ret_norm_g"):
                at = row(l, at, vec(A[k][l]))
            at = row(l, at, A["conv_w"][l].rearrange("w (a b) -> (w a) b", b=128))
            assert at == 94
            row(2, 48 * l, vec(A["b_mod_2"][l]))
        at = 0
        for k in ("norm1_g_2", "norm2_g_2", "q_norm_g_2", "kv_norm_g_2", "hy_short_b_2", "hy_bias_2"):
            for l in range(2):
                at = row(3, at, vec(A[k][l]))
        for k in (A["final_norm"], A["final_g_2"], A["c_2"][0], A["c_ctx_2"]):
            at = row(3, at, vec(k))
        assert at == 106, at
        at = 0
        for l in range(2):
            at = row(4, at, A["hy_short_w_2"][l].rearrange("w (a b) -> (w a) b", b=128))
        assert at == 72

        N_CONST, N_VECTORS = len(CONSTS) + 1, 3 + len(vectors)
        HALF_V = len(vectors) // 2

        @block.sync
        def _(sp):
            def stream(units, p, before):
                for n, (src, kt, nn) in enumerate(units):
                    s = n % RAW
                    if n >= RAW:
                        sp.wait_ge(weight_split, OFF + p.u + n - RAW + 1)
                    else:
                        j = (before - 1) - ((before - 1 - s) % RAW)
                        sp.wait_ge(weight_split, OFF + p.u - before + max(j, 0) + 1)
                    sp.dma_start(raw[:, s, 0:kt * nn].rearrange("p (k n) -> p k n", k=kt), src).then_inc(landed[s], 16)

            sp.dma_start(ident[:, :], A["k_ident"]).then_inc(vectors_in, 16)
            for i, name in enumerate(("x", "ctx_2")):
                sp.dma_start(S[:, TOKENS + i * 2048:TOKENS + (i + 1) * 2048].rearrange("p (a d) -> p a d", a=2),
                             A[name][0].rearrange("(a p) d -> p a d", p=128)).then_inc(vectors_in, 16)
            for dst, src in vectors[:HALF_V]:
                sp.dma_start(dst, src).then_inc(vectors_in, 16)
            with sp.Fori(0, 2) as l:
                p = places1(l)
                w1, w2 = lay(A["ffn1_w_in"], l), lay(A["ffn1_w_out"], l)
                wm = lay(A["w_mod_2"], l)
                stream(ffn_units(w1, w1, FF, w2, (wm, 0)), p["ffn1"], FF1)
                w1, w2 = lay(A["mix_w_in"], l), lay(A["mix_w_out"], l)
                stream([cols(w1, n * 128, 128) for n in range(IN1)], p["in"], FF1)
                stream([cols(w2, n * 128, 128) for n in range(KT)], p["out"], IN1)
                w1, w2 = lay(A["ffn2_w_in"], l), lay(A["ffn2_w_out"], l)
                stream(ffn_units(w1, w1, FF, w2, (wm, MODH * 128)), p["ffn2"], KT)
            before = FF1

            def phase(name, units):
                nonlocal before
                assert sizes2[name] == len(units), name
                stream(units, places2[name], before)
                before = len(units)

            for inst, l, full in MIXES:
                if inst == "c1":
                    for nm in ("ffx", "ffc"):
                        phase(nm, ffn_units(A["ffn_w_gate_2"][0], A["ffn_w_up_2"][0], 0, A["ffn_w_down_2"][0]))
                phase(inst + "in", in2_units(l, full))
                phase(inst + "qkv", qkv_units(l, full))
                if full:
                    phase(inst + "merge", merge_units(l))
                    phase(inst + "out", [cols(A["w_out_2"][l], n * 128, 128) for n in range(KT)])
            sp.wait_ge(weight_split, OFF + moe_at.u)
            sp.wait_ge(plan_ready, 1)
            with sp.Fori(0, sp.value_load(plan[0:1, 32:33], min_val=1, max_val=ITEMS)) as i:
                e = sp.value_load(plan[0:1, bass.ds(i + 16, 1)], min_val=0, max_val=NE - 1)
                wg, wu, wd = (lay(A[k].rearrange("o e k n -> (o e) k n"), e)
                              for k in ("moe_w_gate_2", "moe_w_up_2", "moe_w_down_2"))
                stream(item_units(wg, wu, wd), place_moe(i), FFU)

        NT = 10

        @block.gpsimd
        def _(pool):
            heard = Heard("pool", hs)

            def const(dst, src):
                pool.dma_start(dst, src).then_inc(consts_in, 16)

            for dst, name in CONSTS:
                const(dst, A[name])
            const(rt[:, :, :], A["moe_router_2"][0].rearrange("(k p) e -> p k e", p=128))
            for inst, l, full in MIXES:
                if full:
                    pool.wait_ge(dve_to_pool, heard.next("dve_to_pool"))
                    if inst == "x0":
                        pool.dma_start(S[:, 0:2816], A["k_dft"]).then_inc(table_in, 16)
                        pool.wait_ge(dve_to_pool, heard.next("dve_to_pool"))
                        pool.wait_ge(kept_out, 16)
                        pool.dma_start(S[:, 2816:5376], kept).then_inc(kept_in, 16)
                        continue
                    for a, n, src in ((0, 2816, A["k_dft"]), (8960, 1024, A["hy_w3_2"][l]),
                                      (7936, 1024, A["hy_decay_2"][l].rearrange("a b -> (a b)").partition_broadcast(128)),
                                      (9984, 64, A["hy_w1_2"][l]), (10048, 64, A["hy_w2_2"][l]), (10112, 256, A["k_hyz"]),
                                      (12032, 2, A["k_negt"]),
                                      (10370, 1, A["hy_freq_2"][l].rearrange("(a b) -> a b", b=1)),
                                      (10371, 1, A["hy_b1_2"][l].rearrange("(a b) -> a b", b=1)),
                                      (10372, 1, A["hy_b2_2"][l].rearrange("(a b) -> a b", b=1))):
                        pool.dma_start(S[0:src.shape[0], a:a + n], src).then_inc(table_in, 16)
                    if inst == "c0":
                        pool.wait_ge(act_to_pool, heard.next("act_to_pool"))
                        pool.dma_start(kept, S[:, 2816:5376]).then_inc(kept_out, 16)
            for a in range(2):
                pool.wait_ge(act_to_pool, heard.next("act_to_pool"))
                pool.dma_start(out[0, a * 128:(a + 1) * 128, :], S[:, a * 1024:(a + 1) * 1024]).then_inc(stored, 16)
            pool.wait_ge(stored, 32)

        def bank(h):
            return W[:, h, :] if h < 4 else ACC[:, 2 * (h - 4):2 * (h - 4) + 2, :].rearrange("p a t -> p (a t)")

        SZ, SE, SN, SW = (S[:, i * 3072:(i + 1) * 3072].rearrange("p (h n) -> p h n", h=8) for i in range(4))
        fc, fsn, fs0 = (S[:, i * 512:(i + 1) * 512].rearrange("p (a f) -> p a f", a=2) for i in range(3))
        fcn = S[:, 1536:1792].rearrange("p (a f) -> p a f", a=2)
        ginv = S[:, 1792:2816].rearrange("p (f t) -> p f t", f=4)
        KF = S[:, 2816:5376].rearrange("p (f n) -> p f n", f=5)
        HH = S[:, 5888:7936].rearrange("p (a s n) -> p a s n", a=2, s=2)
        DECAY = S[:, 7936:8960]
        HSUM = S[:, 7936:8960].rearrange("p (a n) -> p a n", a=2)
        w3 = S[0:64, 8960:9984]
        ENV = S[:, 9984:12032].rearrange("p (a s n) -> p a s n", a=2, s=2)
        w1s, w2s, zs = S[0:17, 9984:10048], S[0:64, 10048:10112], S[0:17, 10112:10368]
        fq, b1c, b2c = (S[0:64, c:c + 1] for c in (10370, 10371, 10372))
        negt = S[:, 12032:12034]
        u_s, k_s, s_s = (S[0:64, c:c + 256] for c in (5888, 6144, 6400))
        ZT = S[:, 9984:11008].rearrange("p (a n) -> p a n", a=2)
        YF = S[:, 7936:9984].rearrange("p (f n) -> p f n", f=4)
        TMP = S[:, 11008:12032].rearrange("p (a n) -> p a n", a=2)
        P2 = S[:, 2816:3840].rearrange("p (a n) -> p a n", a=2)
        PT2 = S[:, 3840:4864].rearrange("p (a n) -> p a n", a=2)
        ROT = S[:, 4864:5376].rearrange("p (a t) -> p a t", a=2)
        Y = TT[:, 0:4, :].rearrange("p k t -> p (k t)")
        YP = ACC[:, 0:4, :].rearrange("p k t -> p (k t)")
        TOKhi, TOKlo = (g[:, :, :].rearrange("p (a x) t -> p a (x t)", a=2) for g in (Ghi, Glo))
        GP = ACC[:, 4:8, :].rearrange("p k (x t) -> p (k x) t", x=2)
        rn = small[:, 32:36]

        QKV = lambda full: ([(3, 96)] * 8 if full else []) + [(2, 128)] * 8
        IN2 = lambda full: [(KT, 128)] * (18 if full else 3)
        MERGE = [(KT, 128), (KT, 128), (4, 128), (4, 128)] * KT
        to_in1 = lambda n: "act"
        to_in2 = lambda full: lambda n: "act" if n < (6 if full else 3) else "dve"
        to_merge = lambda n: "act" if n % 4 < 2 else "dve"

        @block.tensor
        def _(pe):
            heard = Heard("pe", hs)
            mm = nc.tensor.matmul

            def f32(o, a, b, start=True, stop=True):
                return mm(o, a, b, start=start, stop=stop, skip_group_check=True)

            def mm3(o, wh, wl, xh, xl, start, stop, swap=False):
                for i, (a, b) in enumerate(((wh, xh), (wh, xl), (wl, xh))):
                    if swap:
                        a, b = b, a
                    last = mm(o, a, b, start=start and i == 0, stop=stop and i == 2, skip_group_check=True)
                return last

            def linear(p, units, x, to, token_major=(), by_tile=False):
                N = len(units)
                for n, (kt, nn) in enumerate(units):
                    pe.wait_ge(weight_split, OFF + p.u + n + 1)
                    if n >= 4:
                        pe.wait_ge(hs[to(n - 4) + "_to_pe"], heard.next(to(n - 4) + "_to_pe"))
                    sl = n % SPLIT
                    xh, xl = x(n)
                    parts = [slice(0, T)] if n not in token_major else [slice(0, 128), slice(128, T)]
                    for ts in parts:
                        for k in range(kt):
                            if by_tile and n == 0:
                                pe.wait_ge(dve_to_pe, heard.next("dve_to_pe"))
                            w_h, w_l = whi[:, sl, k * nn:(k + 1) * nn], wlo[:, sl, k * nn:(k + 1) * nn]
                            o = W[0:nn, n % 4, 0:T] if len(parts) == 1 else W[:, n % 4, ts]
                            last = mm3(o, w_h, w_l, xh[:, k, ts], xl[:, k, ts], k == 0, k == kt - 1, swap=len(parts) > 1)
                    last.then_inc(weight_used, 1)
                for n in range(max(N - 4, 0), N):
                    pe.wait_ge(hs[to(n) + "_to_pe"], heard.next(to(n) + "_to_pe"))

            def norm(kt=KT, squared=False):
                for k in range(kt):
                    if not squared:
                        pe.wait_ge(act_to_pe, heard.next("act_to_pe"))
                    last = f32(W[:, 0, 0:T], ones[:, :], TT[:, k, :], k == 0, k == kt - 1)
                last.then_inc(pe_to_act, 1)

            def ffn(p, riders=False):
                order = FFN_MOD if riders else FFN
                for n, (kind, f) in enumerate(order):
                    pe.wait_ge(weight_split, OFF + p.u + n + 1)
                    sl = n % SPLIT
                    if kind == "down":
                        pe.wait_ge(dve_to_pe, heard.next("dve_to_pe"))
                        for d in range(KT):
                            if riders and f == NF - 1 and d == KT - 1:
                                pe.wait_ge(dve_rows, heard.next("dve_rows"))
                            wh, wl = whi[:, sl, d * 128:(d + 1) * 128], wlo[:, sl, d * 128:(d + 1) * 128]
                            last = mm3(ACC[:, d, :], wh, wl, hhi[:, f % 2, :], hlo[:, f % 2, :],
                                       f == 0 and d % 2 == 0, f == NF - 1)
                    elif kind == "mod":
                        if f % 4 == 0 and f >= 4:
                            pe.wait_ge(dve_rows, heard.next("dve_rows"))
                        for k in range(2):
                            w = slice(k * 512, (k + 1) * 512)
                            c = CS4[:, f % 4 * 2 + k, :]
                            mm(W[0:4, 3, :], c, whi[:, sl, w], start=f % 4 == 0 and k == 0, stop=False,
                               skip_group_check=True)
                            last = mm(W[0:2, 3, :], c[:, 0:2], wlo[:, sl, w], start=False, stop=f % 4 == 3 and k == 1,
                                      skip_group_check=True)
                    else:
                        o = W[:, f % 3, 0:T] if kind == "gate" else W[:, f % 3, T:2 * T]
                        for k in range(KT):
                            if n == 0:
                                pe.wait_ge(dve_to_pe, heard.next("dve_to_pe"))
                            last = mm3(o, whi[:, sl, k * 128:(k + 1) * 128], wlo[:, sl, k * 128:(k + 1) * 128],
                                       Hhi[:, k, :], Hlo[:, k, :], k == 0, k == KT - 1)
                    last.then_inc(weight_used, 1)
                if riders:
                    for n in range(MODH):
                        last = nc.tensor.transpose(W[:, 3, 4 * n:4 * n + 4], MR[0:4, n * 128:(n + 1) * 128], ident[0:4, 0:4])
                    last.then_inc(pe_to_dve, 1)

            def stick_scores(q, k):
                for h in range(8):
                    b, qh, kh = bank(h), q(h), k(h)
                    f32(b[:, 0:256], kh[:, 0:128], qh)
                    last = f32(b[:, 256:384], kh[:, 128:256], qh[:, 128:256])
                last.then_inc(pe_to_act, 1)

            def values(heads, v, w, o):
                for h in range(heads):
                    f32(o(h)[0:64, 0:256], v[:, 0, h * 64:(h + 1) * 64], w[:, h, 0:256], True, False)
                    last = f32(o(h)[0:64, 128:256], v[:, 1, h * 64:(h + 1) * 64], w[:, h, 256:384], False, True)
                last.then_inc(pe_to_act, 1)

            def mix1(p):
                linear(p["in"], [(KT, 128)] * IN1, lambda n: (Hhi, Hlo), to_in1, token_major=(12, 13, 14, 15, 20, 21),
                       by_tile=True)
                side = lambda h: slice(h % 2 * 64, h % 2 * 64 + 64)
                stick_scores(lambda h: QK1[side(h), h // 2, :], lambda h: QK1[side(h), 4 + h // 2, :])
                pe.wait_ge(act_to_pe, heard.next("act_to_pe"))
                for j in range(4):
                    last = f32(W[:, j, 0:T], perm64[:, :], QKR[:, j, :])
                last.then_inc(pe_to_dve, 1)
                pe.wait_ge(dve_to_pe, heard.next("dve_to_pe"))
                for h in range(8):
                    b = bank(h)
                    f32(b[:, 0:256], tri[:, :], SN[:, h, 0:256], True, False)
                    f32(b[:, 128:256], ones[:, :], SN[:, h, 256:384], False, True)
                    last = f32(b[:, 256:384], tri[:, :], SN[:, h, 256:384])
                last.then_inc(pe_to_dve, 1)
                pe.wait_ge(dve_to_pe, heard.next("dve_to_pe"))
                values(8, V1, SW, bank)
                pe.wait_ge(act_to_pe, heard.next("act_to_pe"))
                for h in range(4):
                    q, k = QKR[side(h), h // 2, :], QKR[side(h), 2 + h // 2, :]
                    f32(bank(h)[:, 0:256], k[:, 0:128], q)
                    last = f32(bank(h)[:, 256:384], k[:, 128:256], q[:, 128:256])
                last.then_inc(pe_to_dve, 1)
                pe.wait_ge(dve_to_pe, heard.next("dve_to_pe"))
                values(4, VR, SE, lambda h: bank(4 + h))
                pe.wait_ge(act_to_pe, heard.next("act_to_pe"))
                for i in range(2):
                    f32(W[:, 0, i * T:(i + 1) * T], blk[:, :], TT[:, 6 + i, :])
                for i in range(2):
                    last = f32(W[:, 1, 0:T], ones[:, :], CY[:, i, :], i == 0, i == 1)
                last.then_inc(pe_to_dve, 1)
                pe.wait_ge(act_to_pe, heard.next("act_to_pe"))
                for i in range(2):
                    f32(W[:, 0, i * T:(i + 1) * T], blk[:, :], SE[:, i, 0:T])
                for i in range(2):
                    last = f32(W[:, 1, 0:T], ones[:, :], SE[:, 2 + i, 0:T], i == 0, i == 1)
                last.then_inc(pe_to_act, 1)
                pe.wait_ge(dve_to_pe, heard.next("dve_to_pe"))
                linear(p["out"], [(KT, 128)] * KT, lambda n: (Hhi, Hlo), lambda n: "act")

            def attention(KN):
                nk = KN // 128
                for i in range(16 + 2):
                    if i < 16:
                        h, j = i // 2, i % 2
                        f32(W[:, i % 2, 0:KN], TT[0:96, h, j * 128:(j + 1) * 128], KTt[:, h, 0:KN]
                            ).then_inc(pe_to_dve, 1)
                    if 1 <= i <= 16:
                        pe.wait_ge(dve_to_pe, heard.next("dve_to_pe"))
                        for a in range(nk):
                            last = nc.tensor.transpose(W[:, 2 + (i - 1) % 2, a * 128:(a + 1) * 128],
                                                       P2[:, (i - 1) % 2, a * 128:(a + 1) * 128], ident[:, :])
                        last.then_inc(pe_to_act, 1)
                    if i >= 2:
                        pe.wait_ge(act_to_pe, heard.next("act_to_pe"))
                        h = (i - 2) // 2
                        for a in range(nk):
                            last = f32(ACC[0:64, 2 * (i % 2), 0:128], V2[:, a, h * 64:(h + 1) * 64],
                                       PT2[:, i % 2, a * 128:(a + 1) * 128], a == 0, a == nk - 1)
                        last.then_inc(pe_to_dve, 1)

            tables = 0

            def hyena_filter():
                f32(W[0:64, 0, 0:T], w1s, zs).then_inc(pe_to_dve, 1)
                pe.wait_ge(act_to_pe, heard.next("act_to_pe"))
                f32(W[0:64, 1, 0:T], w2s, s_s).then_inc(pe_to_dve, 1)
                pe.wait_ge(act_to_pe, heard.next("act_to_pe"))
                for a in range(2):
                    for c in range(2):
                        last = f32(W[:, 2 * a + c, :], s_s[:, a * 128:(a + 1) * 128], w3[:, c * 512:(c + 1) * 512])
                last.then_inc(pe_to_dve, 1)
                pe.wait_ge(act_to_pe, heard.next("act_to_pe"))
                for c in range(4):
                    for n in range(4):
                        last = f32(W[:, 0, c:c + 1], ENV[:, n // 2, n % 2, c * 128:(c + 1) * 128], ones[:, 0:1],
                                   n == 0, n == 3)
                last.then_inc(pe_to_dve, 1)
                pe.wait_ge(dve_to_pe, heard.next("dve_to_pe"))
                for f in range(5):
                    table = (fc, fc, fs0, fs0, fcn)[f]
                    o = W[:, 1, :] if f == 4 else bank(4 + f)
                    for a in range(2):
                        last = f32(o, table[:, a, f % 2 * 128:f % 2 * 128 + 128],
                                   HSUM[:, a, :] if f in (0, 1, 4) else HH[:, a, 0, :], a == 0, a == 1)

            def hyena(again):
                nonlocal tables
                tables += 1 if again else NT
                pe.wait_ge(table_in, 16 * tables)
                if again:
                    pe.wait_ge(dve_to_pe, heard.next("dve_to_pe"))
                else:
                    hyena_filter()
                for i in range(4):
                    for a in range(2):
                        last = nc.tensor.transpose(W[:, 2 + a, i * 128:(i + 1) * 128], U[:, i, a * 128:(a + 1) * 128],
                                                   ident[:, :])
                last.then_inc(pe_to_act, 1)
                pe.wait_ge(act_to_pe, heard.next("act_to_pe"))
                for f in range(4):
                    for a in range(2):
                        last = f32(bank(4 + f), (fc, fsn)[f // 2][:, a, f % 2 * 128:f % 2 * 128 + 128], ZT[:, a, :],
                                   a == 0, a == 1)
                last.then_inc(pe_to_dve, 1)
                pe.wait_ge(dve_to_pe, heard.next("dve_to_pe"))
                for c in range(4):
                    for f in range(4):
                        last = f32(W[:, c, 0:T], YF[:, f, c * 128:(c + 1) * 128], ginv[:, f, :], f == 0, f == 3)
                last.then_inc(pe_to_dve, 1)

            def mix2(inst, full):
                x = inst[0] == "x"
                norm()
                linear(places2[inst + "in"], IN2(full), lambda n: (Hhi, Hlo), to_in2(full), by_tile=True)
                for i in range(2 if x else 1):
                    last = f32(W[0:96, 1 + i, 0:T], selk[:, i, :], PQ[:, 5, :])
                last.then_inc(pe_to_dve, 1)
                for kt in ([3] if full else []) + [2]:
                    norm(kt)
                for _ in range(5 if full else 2):
                    pe.wait_ge(dve_to_pe, heard.next("dve_to_pe"))
                linear(places2[inst + "qkv"], QKV(full),
                       lambda n: (Ghi, Glo) if full and n < 8 else (Ghi[:, 3:5, :], Glo[:, 3:5, :]),
                       lambda n: "act", token_major=tuple(range(12 if full else 4, 16 if full else 8)))
                if not full:
                    return
                if x:
                    for h in range(8):
                        last = f32(W[0:96, h // 2, h % 2 * T:h % 2 * T + T], perm96[:, :], TT[0:96, h, :])
                    last.then_inc(pe_to_dve, 1)
                    pe.wait_ge(dve_to_pe, heard.next("dve_to_pe"))
                attention(512 if x else 256)
                hyena(inst == "x0")
                pe.wait_ge(dve_to_pe, heard.next("dve_to_pe"))
                linear(places2[inst + "merge"], MERGE,
                       lambda n: ((Hhi, Hlo), (Hhi, Hlo), (Ghi, Glo), (Ghi[:, 4:8, :], Glo[:, 4:8, :]))[n % 4], to_merge)
                pe.wait_ge(dve_to_pe, heard.next("dve_to_pe"))
                linear(places2[inst + "out"], [(KT, 128)] * KT, lambda n: (Hhi, Hlo), lambda n: "act")

            def gather(tok):
                for k in range(KT):
                    for a in range(2):
                        last = mm(GP[:, k, :], tok[:, a, k * 128:(k + 1) * 128], sel[:, a, :], start=a == 0, stop=a == 1,
                                  skip_group_check=True)
                last.then_inc(pe_to_act, 1)

            def scatter(r):
                for d in range(4):
                    for y in (Yhi, Ylo):
                        at = (4 * r + d) * 128
                        last = mm(ACC[:, 4 + d, :], y[:, at:at + 128], selT[:, :], start=y is Yhi, stop=y is Ylo,
                                  skip_group_check=True)
                last.then_inc(pe_to_dve, 1)

            def turn(g):
                pe.wait_ge(dve_to_pe, heard.next("dve_to_pe"))
                for j in range(GROUPS[g] // 128):
                    at = slice(j * 128, (j + 1) * 128)
                    last = nc.tensor.transpose(W[:, 2 * (g % 2), at], hdt[:, g % 2, at], ident[:, :])
                last.then_inc(pe_to_act, 1)

            def item(p):
                pe.wait_ge(act_to_pe, heard.next("act_to_pe"))
                for n, (kind, g, j) in enumerate(ITEM):
                    parts = GROUPS[g] // 128
                    if kind == "down" and j == 0:
                        if g == NG - 1:
                            pe.wait_ge(act_to_pe, heard.next("act_to_pe"))
                            gather(TOKlo)
                        pe.wait_ge(dve_to_pe, heard.next("dve_to_pe"))
                    pe.wait_ge(weight_split, OFF + p.u + n + 1)
                    sl = n % SPLIT
                    if kind == "down":
                        at = slice(j * 128, (j + 1) * 128)
                        for c in range(2):
                            o = YP[:, c * 512:(c + 1) * 512]
                            w_h, w_l = whi[:, sl, c * 512:(c + 1) * 512], wlo[:, sl, c * 512:(c + 1) * 512]
                            last = mm3(o, w_h, w_l, hgi[:, g % 2, at], hgo[:, g % 2, at], g == 0 and j == 0,
                                       g == NG - 1 and j == parts - 1, swap=True)
                    else:
                        o = W[:, 2 * (g % 2) + (kind == "up"), 0:GROUPS[g]]
                        kt = 1024 // GROUPS[g]
                        for k in range(kt):
                            w = slice(k * GROUPS[g], (k + 1) * GROUPS[g])
                            at = j * kt + k
                            last = mm3(o, whi[:, sl, w], wlo[:, sl, w], Hhi[:, at, 0:128], Hlo[:, at, 0:128],
                                       at == 0, at == KT - 1, swap=True)
                    last.then_inc(weight_used, 1)
                    if kind == "gate" and j == parts - 1 and g >= 1:
                        if g == 1:
                            pe.wait_ge(dve_to_pe, heard.next("dve_to_pe"))
                            scatter(0)
                        turn(g - 1)
                        if g == 2:
                            pe.wait_ge(dve_to_pe, heard.next("dve_to_pe"))
                            scatter(1)
                        if g == 3:
                            pe.wait_ge(dve_to_pe, heard.next("dve_to_pe"))
                            for a in range(2):
                                nc.tensor.transpose(ACC[:, 4, a * 128:(a + 1) * 128], sel[:, a, :].bitcast(F32), ident[:, :])
                            for a in range(2):
                                last = f32(ACC[:, 6, 0:1], sel[:, a, :].bitcast(F32), now[:, 2 + a:3 + a], a == 0, a == 1)
                            last.then_inc(pe_to_act, 1)
                        if g == 4:
                            pe.wait_ge(dve_to_pe, heard.next("dve_to_pe"))
                    if kind == "up" and g == NG - 1 and j == parts - 1:
                        pe.wait_ge(act_to_pe, heard.next("act_to_pe"))
                        gather(TOKhi)
                    if (kind, g, j) == ("down", NG - 2, 1):
                        turn(NG - 1)

            pe.wait_ge(vectors_in, 16 * N_VECTORS)
            pe.wait_ge(consts_in, 16 * N_CONST)
            pe.wait_ge(dve_to_pe, heard.next("dve_to_pe"))
            for k in range(KT):
                for a in range(2):
                    src = TOKENS + a * D + k * 128
                    last = nc.tensor.transpose(ACC[:, k, a * 128:(a + 1) * 128], S[:, src:src + 128], ident[:, :])
            last.then_inc(pe_to_act, 1)
            for t, n in enumerate((94, 94, 96, 106, 72)):
                last = nc.tensor.transpose(W[:, t // 4, t % 4 * 128:t % 4 * 128 + n], rows[0:n, t, :], ident[0:n, 0:n])
            last.then_inc(pe_to_dve, 1)
            pe.wait_ge(dve_to_pe, heard.next("dve_to_pe"))
            for k in range(KT):
                for a in range(2):
                    src = TOKENS + 2048 + a * D + k * 128
                    last = nc.tensor.transpose(W[:, k // 2, k % 2 * T + a * 128:k % 2 * T + a * 128 + 128],
                                               S[:, src:src + 128], ident[:, :])
            last.then_inc(pe_to_act, 1)
            pe.wait_ge(act_to_pe, heard.next("act_to_pe"))
            f32(ACC[:, 0, 0:2], ones[:, :], CS[:, 0, :]).then_inc(weight_used, OFF)
            with pe.Fori(0, 2) as l:
                heard.enter("layers", l)
                p = places1(l)
                norm()
                ffn(p["ffn1"], riders=True)
                norm()
                mix1(p)
                norm(squared=True)
                ffn(p["ffn2"], riders=True)
                heard.leave("layers", 2)
            norm()
            for inst, l, full in MIXES:
                if inst == "c1":
                    for name in ("ffx", "ffc"):
                        norm(squared=name == "ffx")
                        ffn(places2[name])
                mix2(inst, full)
            norm(squared=True)
            for _ in range(KT):
                pe.wait_ge(dve_to_pe, heard.next("dve_to_pe"))
            for a in range(2):
                for k in range(KT):
                    for i, h in enumerate((Hhi, Hlo)):
                        last = f32(W[:, 0, a * NE:(a + 1) * NE], h[:, k, a * 128:(a + 1) * 128].bitcast(F32), rt[:, k, :],
                                   k == 0 and i == 0, k == KT - 1 and i == 1)
            last.then_inc(pe_to_dve, 1)
            pe.wait_ge(dve_to_pe, heard.next("dve_to_pe"))
            for i, h in enumerate((Hhi, Hlo)):
                for a in range(2):
                    for k in range(KT):
                        at = a * D + k * 128
                        dst = W[:, at // 512, at % 512:at % 512 + 128] if i == 0 else ACC[:, at // T, at % T:at % T + 128]
                        last = nc.tensor.transpose(dst, h[:, k, a * 128:(a + 1) * 128].bitcast(F32), ident[:, :])
                last.then_inc(pe_to_act, 1)
            pe.wait_ge(act_to_pe, heard.next("act_to_pe"))
            pe.wait_ge(dve_to_pe, heard.next("dve_to_pe"))
            taken = route[:, 4, 0:16].rearrange("p (a e) -> p a e", a=2)
            f32(W[:, 0, 0:8], mask[:, 0:128], taken[:, 0, :])
            f32(W[:, 0, 8:16], ones[:, :], taken[:, 0, :], True, False)
            f32(W[:, 0, 8:16], mask[:, 0:128], taken[:, 1, :], False, True)
            f32(W[:, 0, 16:24], ones[:, :], taken[:, 0, :], True, False)
            f32(W[:, 0, 16:24], ones[:, :], taken[:, 1, :], False, True).then_inc(pe_to_dve, 1)
            pe.wait_ge(dve_to_pe, heard.next("dve_to_pe"))
            for c in range(4):
                last = mm(ACC[:, c, :], selT[:, 0:128], selT[:, :], start=c % 2 == 0, stop=True, skip_group_check=True)
            last.then_inc(pe_to_dve, 1)
            gather(TOKhi)
            pe.wait_ge(act_to_pe, heard.next("act_to_pe"))
            gather(TOKlo)
            pe.wait_ge(plan_ready, 1)
            n_items = pe.value_load(plan[0:1, 32:33], min_val=1, max_val=ITEMS)
            with pe.Fori(0, n_items) as i:
                heard.enter("items", i)
                item(place_moe(i))
                heard.leave("items", n_items)
            pe.wait_ge(act_to_pe, heard.next("act_to_pe"))
            for r in range(2):
                pe.wait_ge(dve_to_pe, heard.next("dve_to_pe"))
                scatter(r)
            norm()
            pe.wait_ge(dve_to_pe, heard.next("dve_to_pe"))
            for a in range(2):
                for k in range(KT):
                    last = nc.tensor.transpose(W[:, 2 * a + k // 4, k % 4 * 128:k % 4 * 128 + 128],
                                               TT[:, k, a * 128:(a + 1) * 128], ident[:, :])
                last.then_inc(pe_to_act, 1)

        def splitter(eng, one_unit, units):
            at = [0]

            def upto(n):
                while at[0] < min(n, len(units)):
                    one_unit(at[0], units[at[0]])
                    at[0] += 1
            return upto

        LEAD = 4

        @block.scalar
        def _(act):
            heard = Heard("act", hs)
            A_ = nc.scalar.activation

            def link(ins):
                ins.then_inc(act_done, 1)
                act.wait_ge(act_done, heard.next("act_done"))

            def tell(name):
                A_(small[0:1, 50:51], small[0:1, 51:52], ACT.Copy)
                act.drain().then_inc(hs[name], 1)

            def split_units(p, units):
                def one_unit(n, size):
                    w, s, sl = size, n % RAW, n % SPLIT
                    act.wait_ge(landed[s], 16 * (p.land[s] + n // RAW + 1))
                    act.wait_ge(weight_used, OFF + p.u + (n - SPLIT + 1 if n >= SPLIT else 0))
                    A_(whi[:, sl, 0:w], raw[:, s, 0:w], ACT.Copy).then_inc(weight_high, 1)
                return splitter(act, one_unit, units)

            def linear(p, units, to, evac):
                upto = split_units(p, [a * b for a, b in units])
                upto(LEAD)
                for n in range(len(units)):
                    upto(n + 1 + LEAD)
                    if to(n) == "act":
                        act.wait_ge(weight_used, OFF + p.u + n + 1)
                        evac(n, W[:, n % 4, :]).then_inc(act_to_pe, 1)

            def norm(src, kt=KT, shift=None, dst=None, at=0, after="one"):
                if after == "one":
                    act.wait_ge(dve_to_act, heard.next("dve_to_act"))
                for k in range(kt if after != "squared" else 0):
                    if after == "tiles":
                        act.wait_ge(dve_to_act, heard.next("dve_to_act"))
                    A_(TT[:, k, :], src[:, k, :], ACT.Square).then_inc(act_to_pe, 1)
                act.wait_ge(pe_to_act, heard.next("pe_to_act"))
                A_(R[:, :], W[:, 0, 0:T], ACT.Sqrt, bias=epsc, scale=1.0 / (kt * 128)).then_inc(act_to_dve, 1)
                if dst is not None:
                    for k in range(kt):
                        act.wait_ge(dve_to_act, heard.next("dve_to_act"))
                        A_(dst[:, at + k, :], TT[:, k, :], ACT.Identity,
                           bias=zeroc if shift is None else shift(k)).then_inc(act_to_dve, 1)

            def hidden(p, order):
                N = len(order)
                at = AT[N]

                def one_unit(n, w):
                    s, sl = n % RAW, n % SPLIT
                    act.wait_ge(landed[s], 16 * (p.land[s] + n // RAW + 1))
                    act.wait_ge(weight_used, OFF + p.u + (n - SPLIT + 1 if n >= SPLIT else 0))
                    A_(whi[:, sl, 0:w], raw[:, s, 0:w], ACT.Copy).then_inc(weight_high, 1)

                def high(f):
                    act.wait_ge(dve_to_act, heard.next("dve_to_act"))
                    if f >= 2:
                        act.wait_ge(weight_used, OFF + p.u + at[("down", f - 2)] + 1)
                    A_(hhi[:, f % 2, 0:T], hd[:, f % 3, 0:T], ACT.Copy).then_inc(act_to_dve, 1)

                upto = splitter(act, one_unit, [1024] * N)
                upto(SPLIT)
                for f in range(NF):
                    n = at[("up", f)]
                    act.wait_ge(weight_used, OFF + p.u + n + 1)
                    A_(sg[:, f % 2, 0:T], W[:, f % 3, 0:T], ACT.Silu).then_inc(act_to_dve, 1)
                    upto(n + SPLIT - 1)
                    if f >= 1:
                        high(f - 1)
                    upto(n + SPLIT + 1)
                high(NF - 1)
                upto(N)

            def ffn(p, riders=False):
                hidden(p, FFN_MOD if riders else FFN)

            def mix1(p):
                def evac(n, b):
                    if n < 2:
                        return A_(CA[:, n, :], b[:, 0:T], ACT.Copy)
                    if n < 4:
                        return A_(CB[:, n - 2, :], b[:, 0:T], ACT.Sigmoid)
                    if n < 12:
                        return A_(QK1[:, n - 4, :], b[:, 0:T], ACT.Copy)
                    if n < 16:
                        return A_(V1[:, :, (n - 12) * 128:(n - 11) * 128], b[:, 0:T].rearrange("p (a n) -> p a n", a=2), ACT.Copy)
                    if n < 20:
                        return A_(QKR[:, n - 16, :], b[:, 0:T], ACT.Copy)
                    if n < 22:
                        return A_(VR[:, :, (n - 20) * 128:(n - 19) * 128], b[:, 0:T].rearrange("p (a n) -> p a n", a=2), ACT.Copy)
                    return A_(GR[:, n - 22, :], b[:, 0:T], ACT.Silu)

                upto = split_units(p["in"], [1024] * IN1)
                upto(LEAD)
                for n in range(IN1):
                    upto(n + 1 + LEAD)
                    act.wait_ge(weight_used, OFF + p["in"].u + n + 1)
                    evac(n, W[:, n % 4, :]).then_inc(act_to_pe, 1)
                    if n == 3:
                        tell("act_to_dve")
                act.wait_ge(pe_to_act, heard.next("pe_to_act"))
                for h in range(8):
                    A_(SZ[:, h, :], bank(h)[:, 0:384], ACT.Copy, scale=0.125)
                tell("act_to_pe")
                tell("act_done")
                act.wait_ge(act_done, heard.next("act_done"))
                link(A_(SE[:, :, :], SZ[:, :, :], ACT.Abs))
                link(A_(SE[:, :, :], SE[:, :, :], ACT.Exp, scale=-1.0))
                A_(SE[:, :, :], SE[:, :, :], ACT.Ln, bias=onec).then_inc(act_to_dve, 1)
                act.wait_ge(dve_to_act, heard.next("dve_to_act"))
                A_(SW[:, :, :], SW[:, :, :], ACT.Exp).then_inc(act_to_dve, 1)
                act.wait_ge(pe_to_act, heard.next("pe_to_act"))
                for h in range(8):
                    A_(TT[h % 2 * 64:h % 2 * 64 + 64, 2 + h // 2, :], bank(h)[0:64, 0:T], ACT.Copy)
                tell("act_to_pe")
                act.wait_ge(pe_to_act, heard.next("pe_to_act"))
                for h in range(4):
                    A_(TT[h % 2 * 64:h % 2 * 64 + 64, 6 + h // 2, :], bank(4 + h)[0:64, 0:T], ACT.Copy)
                tell("act_to_pe")
                act.wait_ge(dve_to_act, heard.next("dve_to_act"))
                for i in range(2):
                    A_(SE[:, i, 0:T], TT[:, 6 + i, :], ACT.Square)
                    A_(SE[:, 2 + i, 0:T], CY[:, i, :], ACT.Square)
                tell("act_to_pe")
                act.wait_ge(pe_to_act, heard.next("pe_to_act"))
                A_(SN[:, 0:2, 0:T], W[:, 0, :].rearrange("p (a t) -> p a t", a=2), ACT.Sqrt, bias=epsc)
                A_(SN[:, 2, 0:T], W[:, 1, 0:T], ACT.Sqrt, bias=epsc, scale=1.0 / 256)
                tell("act_to_dve")
                act.wait_ge(dve_to_act, heard.next("dve_to_act"))
                for i in range(2):
                    A_(TT[:, i, :], CY[:, i, :], ACT.Silu, bias=PL[:, 28 + i:29 + i])
                tell("act_done")
                act.wait_ge(act_done, heard.next("act_done"))
                split_x(TT, 0, Hhi, 0, 8)
                out_and_square(p["out"], X)

            def out_and_square(p, res):
                def evac(n, b):
                    act.wait_ge(dve_to_act, heard.next("dve_to_act"))
                    return A_(TT[:, n, :], res[:, n, :], ACT.Square)

                linear(p, [(KT, 128)] * KT, lambda n: "act", evac)

            def split_x(src, a, dst, b, n):
                A_(dst[:, b:b + n, :], src[:, a:a + n, :], ACT.Copy).then_inc(act_to_dve, 1)

            def attention(KN):
                for i in range(17):
                    if i < 16:
                        act.wait_ge(dve_to_act, heard.next("dve_to_act"))
                        c = i % 2 * 4
                        A_(P2[:, i % 2, 0:KN], W[:, i % 2, 0:KN], ACT.Exp, bias=small[:, c:c + 1], scale=SCALE,
                           accum_out=small[:, c + 1:c + 2]).then_inc(act_to_dve, 1)
                    if i >= 1:
                        act.wait_ge(pe_to_act, heard.next("pe_to_act"))
                        A_(PT2[:, (i - 1) % 2, 0:KN], W[:, 2 + (i - 1) % 2, 0:KN], ACT.Copy).then_inc(act_to_pe, 1)

            def hyena_filter():
                for _ in range(2):
                    act.wait_ge(dve_to_act, heard.next("dve_to_act"))
                    A_(s_s, u_s, ACT.Sin).then_inc(act_to_pe, 1)
                act.wait_ge(dve_to_act, heard.next("dve_to_act"))
                link(A_(DECAY, DECAY, ACT.Abs))
                for a in range(2):
                    A_(ENV[:, a, :, :].rearrange("p s n -> p (s n)"), DECAY, ACT.Exp, scale=negt[:, a:a + 1])
                tell("act_to_dve")
                act.wait_ge(dve_to_act, heard.next("dve_to_act"))
                A_(ENV[:, :, :, :], HH[:, :, :, :], ACT.Abs).then_inc(act_to_pe, 1)

            def hyena(inst):
                if inst != "x0":
                    hyena_filter()
                act.wait_ge(pe_to_act, heard.next("pe_to_act"))
                if inst != "x0":
                    for f in range(5):
                        A_(KF[:, f, :], W[:, 1, :] if f == 4 else bank(4 + f), ACT.Copy)
                A_(ZT[:, :, :], W[:, 2:4, :], ACT.Copy)
                tell("act_to_pe")
                if inst == "c0":
                    tell("act_to_pool")
                    act.wait_ge(kept_out, 16)

            def mix2(inst, full, l):
                x = inst[0] == "x"
                st = 0 if x else 1
                t0 = T if x else 0
                norm(X if x else C, shift=lambda k: MOD[:, l, k, st:st + 1], dst=Hhi)

                def evac_in(n, b):
                    return A_(PQ[:, n if full else n + 3, :], b[:, 0:T], ACT.Copy)

                linear(places2[inst + "in"], IN2(full), to_in2(full), evac_in)
                tell("act_done")
                act.wait_ge(act_done, heard.next("act_done"))
                if full:
                    norm(PQ, 3, dst=Ghi, after="self")
                norm(PQ[:, 3:5, :], 2, dst=Ghi, at=3, after="one" if full else "self")

                def evac_qkv(n, b):
                    if full and n < 8:
                        return A_(TT[0:96, n, :], b[0:96, 0:T], ACT.Copy)
                    n -= 8 if full else 0
                    if n < 4:
                        A_(KTt[0:64, 2 * n, t0:t0 + T], b[0:64, 0:T], ACT.Copy)
                        return A_(KTt[0:64, 2 * n + 1, t0:t0 + T], b[64:128, 0:T], ACT.Copy)
                    n -= 4
                    return A_(V2[:, t0 // 128:t0 // 128 + 2, n * 128:(n + 1) * 128],
                              b[:, 0:T].rearrange("p (a n) -> p a n", a=2), ACT.Copy)

                linear(places2[inst + "qkv"], QKV(full), lambda n: "act", evac_qkv)
                if not full:
                    return
                attention(512 if x else 256)
                hyena(inst)
                act.wait_ge(dve_to_act, heard.next("dve_to_act"))
                split_x(PQ, 0, Ghi, 0, 4)
                split_x(U, 4, Ghi, 4, 4)

                def evac_merge(n, b):
                    j, w = n // 4, n % 4
                    return A_(PQ[:, (4, 2)[j % 2] + w, :], b[:, 0:T], ACT.Sigmoid)

                p = places2[inst + "merge"]
                upto = split_units(p, [a * b for a, b in MERGE])
                upto(LEAD)
                for n in range(len(MERGE)):
                    upto(n + 1 + LEAD)
                    if to_merge(n) == "act":
                        act.wait_ge(weight_used, OFF + p.u + n + 1)
                        evac_merge(n, W[:, n % 4, :]).then_inc(act_to_pe, 1)
                        if n % 4 == 1:
                            tell("act_to_dve")
                act.wait_ge(dve_to_act, heard.next("dve_to_act"))
                split_x(TT, 0, Hhi, 0, 8)
                out_and_square(places2[inst + "out"], X if x else C)
                if not x:
                    tell("act_done")
                    act.wait_ge(act_done, heard.next("act_done"))

            def split_rows():
                act.wait_ge(dve_to_act, heard.next("dve_to_act"))
                A_(Yhi[:, :], Y, ACT.Copy).then_inc(act_to_dve, 1)

            def item(p):
                at = {x: n for n, x in enumerate(ITEM)}

                def one_unit(n, w):
                    s, sl = n % RAW, n % SPLIT
                    act.wait_ge(landed[s], 16 * (p.land[s] + n // RAW + 1))
                    act.wait_ge(weight_used, OFF + p.u + n - SPLIT + 1)
                    A_(whi[:, sl, 0:w], raw[:, s, 0:w], ACT.Copy).then_inc(weight_high, 1)

                def high(g):
                    act.wait_ge(pe_to_act, heard.next("pe_to_act"))
                    A_(hgi[:, g % 2, 0:GROUPS[g]], W[:, 2 * (g % 2), 0:GROUPS[g]], ACT.Copy).then_inc(act_to_dve, 1)

                upto = splitter(act, one_unit, [1024] * FFU)
                upto(SPLIT - 1)
                split_rows()
                for g in range(NG):
                    n = at[("gate", g, GROUPS[g] // 128 - 1)]
                    upto(n + SPLIT)
                    act.wait_ge(weight_used, OFF + p.u + n + 1)
                    if g >= 1:
                        high(g - 1)
                    A_(sgt[:, g % 2, 0:GROUPS[g]], W[:, 2 * (g % 2), 0:GROUPS[g]], ACT.Silu).then_inc(act_to_dve, 1)
                    if g == 3:
                        upto(n + SPLIT + 1)
                        act.wait_ge(pe_to_act, heard.next("pe_to_act"))
                        A_(now[:, 4:5], ACC[:, 6, 0:1], ACT.Copy)
                        A_(selT[:, :], ACC[:, 4, :], ACT.Copy)
                        tell("act_to_pe")
                n = at[("up", NG - 1, GROUPS[NG - 1] // 128 - 1)]
                upto(n + SPLIT)
                act.wait_ge(pe_to_act, heard.next("pe_to_act"))
                A_(Hhi[:, :, 0:128], GP, ACT.Copy).then_inc(act_to_pe, 1)
                upto(FFU)
                high(NG - 1)
                act.wait_ge(pe_to_act, heard.next("pe_to_act"))
                A_(Hlo[:, :, 0:128], GP, ACT.Copy).then_inc(act_to_pe, 1)

            for dst, src in vectors[HALF_V:]:
                act.dma_start(dst, src).then_inc(vectors_in, 16)
            act.wait_ge(pe_to_act, heard.next("pe_to_act"))
            for b in range(4):
                A_(X[:, 2 * b:2 * b + 2, :], ACC[:, 2 * b:2 * b + 2, :], ACT.Copy)
            act.wait_ge(dve_to_act, heard.next("dve_to_act"))
            for i in range(2):
                link(A_(CS[:, :, i], PV[:, 3, 90 + 8 * i:98 + 8 * i], ACT.Silu))
            A_(CS4[:, :, 0:2], CS[:, :, :], ACT.Copy).then_inc(act_to_dve, 1)
            act.wait_ge(pe_to_act, heard.next("pe_to_act"))
            for b in range(4):
                A_(C[:, 2 * b:2 * b + 2, :], W[:, b, :].rearrange("p (k t) -> p k t", k=2), ACT.Copy)
            tell("act_to_pe")
            tell("act_done")
            act.wait_ge(act_done, heard.next("act_done"))
            with act.Fori(0, 2) as l:
                heard.enter("layers", l)
                p = places1(l)
                norm(X, dst=Hhi)
                ffn(p["ffn1"], riders=True)
                norm(X, dst=Hhi, after="tiles")
                mix1(p)
                norm(X, dst=Hhi, after="squared")
                ffn(p["ffn2"], riders=True)
                heard.leave("layers", 2)
            norm(X)
            for inst, l, full in MIXES:
                if inst == "c1":
                    for name, st, src in (("ffx", 0, X), ("ffc", 1, C)):
                        norm(src, shift=lambda k: MOD[:, 0, 24 + k, st:st + 1], dst=Hhi,
                             after="one" if st else "squared")
                        ffn(places2[name])
                mix2(inst, full, l)
            norm(X, shift=lambda k: MOD[:, 1, 24 + k, 0:1], dst=Hhi, after="squared")
            act.wait_ge(dve_to_act, heard.next("dve_to_act"))
            A_(route[:, 1, 0:16], route[:, 1, 0:16], ACT.Exp).then_inc(act_to_dve, 1)
            for o, dst in ((W, TOKhi), (ACC, TOKlo)):
                act.wait_ge(pe_to_act, heard.next("pe_to_act"))
                for b in range(4):
                    A_(dst[:, b // 2, b % 2 * 512:b % 2 * 512 + 512],
                       W[:, b, :] if o is W else ACC[:, 2 * b:2 * b + 2, :].rearrange("p k t -> p (k t)"), ACT.Copy)
            tell("act_to_pe")
            for dst in (Hhi, Hlo):
                act.wait_ge(pe_to_act, heard.next("pe_to_act"))
                A_(dst[:, :, 0:128], GP, ACT.Copy).then_inc(act_to_pe, 1)
            act.wait_ge(plan_ready, 1)
            n_items = act.value_load(plan[0:1, 32:33], min_val=1, max_val=ITEMS)
            with act.Fori(0, n_items) as i:
                heard.enter("items", i)
                item(place_moe(i))
                heard.leave("items", n_items)
            split_rows()
            norm(X)
            for a in range(2):
                act.wait_ge(pe_to_act, heard.next("pe_to_act"))
                for b in range(2):
                    A_(S[:, a * 1024 + b * 512:a * 1024 + b * 512 + 512], W[:, 2 * a + b, :], ACT.Copy)
                tell("act_to_pool")

        @block.vector
        def _(dve):
            heard = Heard("dve", hs)
            V = nc.vector

            def link(ins):
                ins.then_inc(dve_done, 1)
                dve.wait_ge(dve_done, heard.next("dve_done"))

            def tell(name):
                V.memset(small[0:1, 48:49], 0.0)
                dve.drain().then_inc(hs[name], 1)

            def settle():
                tell("dve_done")
                dve.wait_ge(dve_done, heard.next("dve_done"))

            def split_units(p, units):
                def one_unit(n, w):
                    s, sl = n % RAW, n % SPLIT
                    dve.wait_ge(weight_high, p.u + n + 1)
                    V.tensor_tensor(wlo[:, sl, 0:w], raw[:, s, 0:w], whi[:, sl, 0:w].bitcast(F32), ALU.subtract
                                    ).then_inc(weight_split, 1)
                return splitter(dve, one_unit, units)

            def linear(p, units, to, evac, extra=None):
                upto = split_units(p, [a * b for a, b in units])
                upto(LEAD)
                for n in range(len(units)):
                    upto(n + 1 + LEAD)
                    if to(n) == "dve":
                        dve.wait_ge(weight_used, OFF + p.u + n + 1)
                        evac(n, W[:, n % 4, :])
                    if extra is not None:
                        extra(n)

            def norm(src, gain, kt=KT, shift=None, hi=None, lo=None, at=0, to=None, told=False):
                if not told:
                    tell("dve_to_act")
                dve.wait_ge(act_to_dve, heard.next("act_to_dve"))
                link(V.reciprocal(R[:, :], R[:, :]))
                def low(k):
                    dve.wait_ge(act_to_dve, heard.next("act_to_dve"))
                    V.scalar_tensor_tensor(lo[:, at + k, :], TT[:, k, :], 0.0 if shift is None else shift(k),
                                           hi[:, at + k, :].bitcast(F32), ALU.add, ALU.subtract).then_inc(dve_to_pe, 1)

                for k in range(kt):
                    ins = V.scalar_tensor_tensor((TT if to is None else to)[:, k, :], src[:, k, :], gain(k), R[:, :],
                                                 ALU.mult, ALU.mult)
                    if hi is not None:
                        ins.then_inc(dve_to_act, 1)
                        if k >= 1:
                            low(k - 1)
                if hi is None:
                    settle()
                else:
                    low(kt - 1)

            def hidden(p, order):
                N = len(order)
                at = AT[N]
                upto = split_units(p, [1024] * N)

                def rows_out(g):
                    dve.wait_ge(weight_used, OFF + p.u + at[("mod", 4 * g + 3)] + 1)
                    V.tensor_copy(MR[0:4, g * 512:(g + 1) * 512], W[0:4, 3, :]).then_inc(dve_rows, 1)

                def low(f):
                    dve.wait_ge(act_to_dve, heard.next("act_to_dve"))
                    V.tensor_tensor(hlo[:, f % 2, 0:T], hd[:, f % 3, 0:T], hhi[:, f % 2, 0:T].bitcast(F32),
                                    ALU.subtract).then_inc(dve_to_pe, 1)

                upto(SPLIT)
                for f in range(NF):
                    n = at[("up", f)]
                    dve.wait_ge(act_to_dve, heard.next("act_to_dve"))
                    V.tensor_tensor(hd[:, f % 3, 0:T], sg[:, f % 2, 0:T], W[:, f % 3, T:2 * T],
                                    ALU.mult).then_inc(dve_to_act, 1)
                    upto(n + SPLIT - 1)
                    if f >= 1:
                        low(f - 1)
                    upto(n + SPLIT + 1)
                    if order is FFN_MOD and f % 4 == 3:
                        rows_out(f // 4)
                low(NF - 1)
                upto(N)
                if order is FFN_MOD:
                    rows_out(NF // 4)

            def ffn(p, gate, res, riders=None, tiles=True):
                order = FFN if riders is None else FFN_MOD
                hidden(p, order)
                dve.wait_ge(weight_used, OFF + p.u + len(order))
                for n in range(KT):
                    ins = V.scalar_tensor_tensor(res[:, n, :], ACC[:, n, :], gate(n), res[:, n, :], ALU.mult, ALU.add)
                    if tiles:
                        ins.then_inc(dve_to_act, 1)
                if riders is not None:
                    half = slice(MODH * riders, MODH * riders + MODH)
                    dve.wait_ge(pe_to_dve, heard.next("pe_to_dve"))
                    got = W[:, 3, 0:4 * MODH].rearrange("p (n i s) -> p n i s", i=2, s=2)
                    link(V.tensor_tensor(ML[:, half, :], got[:, :, 0, :], BL[:, half].unsqueeze(2).broadcast_to([128, MODH, 2]),
                                         ALU.add))
                    link(V.tensor_tensor(ML[:, half, :], ML[:, half, :], got[:, :, 1, :], ALU.add))

            def split_lo(src, a, hi, lo, b, n):
                dve.wait_ge(act_to_dve, heard.next("act_to_dve"))
                return V.tensor_tensor(lo[:, b:b + n, :], src[:, a:a + n, :], hi[:, b:b + n, :].bitcast(F32), ALU.subtract)

            def rotate(dst, src, swapped, cos, sin, tmp):
                V.tensor_tensor(tmp[0], src, cos, ALU.mult)
                link(V.tensor_tensor(tmp[1], swapped, sin, ALU.mult))
                V.tensor_tensor(dst, tmp[0], tmp[1], ALU.add)

            def mix1(p):
                taps = []
                for j in range(CONV_W):
                    for i in range(2):
                        taps.append((j, i))

                def conv(n):
                    if n == 3:
                        dve.wait_ge(act_to_dve, heard.next("act_to_dve"))
                        link(V.tensor_tensor(VP[:, :, 30:30 + T], CA[:, :, :], CB[:, :, :], ALU.mult))
                    if n >= 4:
                        for j, i in taps[4 * (n - 4):4 * (n - 3)]:
                            w = PL[:, 32 + 2 * j + i:33 + 2 * j + i]
                            if j == 0:
                                V.tensor_scalar(CY[:, i, :], VP[:, i, 0:T], w, PL[:, 24 + i:25 + i], ALU.mult, ALU.add)
                            else:
                                V.scalar_tensor_tensor(CY[:, i, :], VP[:, i, j:j + T], w, CY[:, i, :], ALU.mult, ALU.add)
                            if i == 1:
                                settle()

                linear(p["in"], [(KT, 128)] * IN1, to_in1, None, conv)
                dve.wait_ge(pe_to_dve, heard.next("pe_to_dve"))
                for j in range(4):
                    rotate(QKR[:, j, :], QKR[:, j, :], W[:, j, 0:T], rcos, rsin, (SW[:, j, 0:T], SW[:, 4 + j, 0:T]))
                dve.wait_ge(act_to_dve, heard.next("act_to_dve"))
                link(V.scalar_tensor_tensor(SN[:, :, :], SZ[:, :, :], 0.0, SE[:, :, :], ALU.max, ALU.add))
                link(V.tensor_tensor(SZ[:, :, :], SZ[:, :, :], SN[:, :, :], ALU.subtract))
                maskb = mask[:, :].unsqueeze(1).broadcast_to([128, 8, 384])
                link(V.tensor_tensor(SN[:, :, :], SN[:, :, :], maskb, ALU.mult))
                tell("dve_to_pe")
                dve.wait_ge(pe_to_dve, heard.next("pe_to_dve"))
                for h in range(8):
                    V.tensor_tensor(SW[:, h, :], SZ[:, h, :], bank(h)[:, 0:384], ALU.subtract)
                tell("dve_to_act")
                dve.wait_ge(act_to_dve, heard.next("act_to_dve"))
                V.tensor_tensor(SW[:, :, :], SW[:, :, :], maskb, ALU.mult).then_inc(dve_to_pe, 1)
                dve.wait_ge(pe_to_dve, heard.next("pe_to_dve"))
                for h in range(4):
                    V.tensor_tensor(SE[:, h, :], bank(h)[:, 0:384], DR[:, h, :], ALU.mult)
                tell("dve_to_pe")
                dve.wait_ge(pe_to_dve, heard.next("pe_to_dve"))
                for i in range(2):
                    V.tensor_tensor(TT[:, 6 + i, :], TT[:, 6 + i, :], W[:, 0, i * T:(i + 1) * T], ALU.subtract)
                    V.scalar_tensor_tensor(CY[:, i, :], W[:, 1, 0:T], -1.0 / 256, CY[:, i, :], ALU.mult, ALU.add)
                tell("dve_to_act")
                dve.wait_ge(act_to_dve, heard.next("act_to_dve"))
                link(V.reciprocal(SN[:, 0:3, 0:T], SN[:, 0:3, 0:T]))
                for i in range(2):
                    V.scalar_tensor_tensor(CY[:, i, :], CY[:, i, :], PL[:, 26 + i:27 + i], SN[:, 2, 0:T], ALU.mult, ALU.mult)
                    V.tensor_tensor(TT[:, 6 + i, :], TT[:, 6 + i, :], SN[:, i, 0:T], ALU.mult)
                settle()
                for i in range(2):
                    V.scalar_tensor_tensor(TT[:, 6 + i, :], TT[:, 6 + i, :], PL[:, 30 + i:31 + i], GR[:, i, :],
                                           ALU.mult, ALU.mult)
                tell("dve_to_act")
                split_lo(TT, 0, Hhi, Hlo, 0, 8).then_inc(dve_to_pe, 1)

                def evac(n, b):
                    V.tensor_tensor(X[:, n, :], X[:, n, :], b[:, 0:T], ALU.add).then_inc(dve_to_act, 1)

                linear(p["out"], [(KT, 128)] * KT, lambda n: "dve", evac)

            def attention(KN, OA):
                for i in range(18):
                    c = i % 2 * 4
                    if i < 16:
                        dve.wait_ge(pe_to_dve, heard.next("pe_to_dve"))
                        link(V.tensor_reduce(small[:, c + 2:c + 3], W[:, i % 2, 0:KN], AX.X, ALU.max))
                        V.tensor_scalar(small[:, c:c + 1], small[:, c + 2:c + 3], -SCALE, None, ALU.mult
                                        ).then_inc(dve_to_act, 1)
                    if i >= 2:
                        dve.wait_ge(pe_to_dve, heard.next("pe_to_dve"))
                        h, j = (i - 2) // 2, i % 2
                        V.tensor_copy(OA[h % 2 * 64:h % 2 * 64 + 64, h // 2, j * 128:(j + 1) * 128],
                                      ACC[0:64, 2 * (i % 2), 0:128])
                    if i < 16:
                        dve.wait_ge(act_to_dve, heard.next("act_to_dve"))
                        link(V.reciprocal(small[:, c + 3:c + 4], small[:, c + 1:c + 2]))
                        V.tensor_scalar(P2[:, i % 2, 0:KN], P2[:, i % 2, 0:KN], small[:, c + 3:c + 4], None, ALU.mult
                                        ).then_inc(dve_to_pe, 1)

            tables = 0

            def sine_argument(b, o):
                link(V.tensor_scalar(u_s, o, b, fq, ALU.add, ALU.mult))
                link(V.tensor_scalar(k_s, u_s, 1.0 / (2 * math.pi), ROUND, ALU.mult, ALU.add))
                link(V.tensor_scalar(k_s, k_s, ROUND, None, ALU.subtract))
                link(V.scalar_tensor_tensor(u_s, k_s, -TWO_PI_HI, u_s, ALU.mult, ALU.add))
                link(V.scalar_tensor_tensor(u_s, k_s, -TWO_PI_LO, u_s, ALU.mult, ALU.add))
                V.tensor_scalar(u_s, u_s, PI_BELOW, -PI_BELOW, ALU.min, ALU.max).then_inc(dve_to_act, 1)

            def hyena_filter():
                dve.wait_ge(pe_to_dve, heard.next("pe_to_dve"))
                sine_argument(b1c, W[0:64, 0, 0:T])
                dve.wait_ge(pe_to_dve, heard.next("pe_to_dve"))
                sine_argument(b2c, W[0:64, 1, 0:T])
                dve.wait_ge(pe_to_dve, heard.next("pe_to_dve"))
                tell("dve_to_act")
                dve.wait_ge(act_to_dve, heard.next("act_to_dve"))
                for a in range(2):
                    for s in range(2):
                        V.tensor_tensor(HH[:, a, s, :], W[:, 2 * a + s, :], ENV[:, a, s, :], ALU.mult)
                settle()
                link(V.memset(HH[0:1, 0, 1, :], 0.0))
                tell("dve_to_act")
                dve.wait_ge(pe_to_dve, heard.next("pe_to_dve"))
                V.reciprocal(rn, W[:, 0, 0:4])
                V.tensor_tensor(HSUM[:, :, :], HH[:, :, 0, :], HH[:, :, 1, :], ALU.add)
                settle()
                V.tensor_tensor(HH[:, :, 0, :], HH[:, :, 0, :], HH[:, :, 1, :], ALU.subtract).then_inc(dve_to_pe, 1)

            def hyena(l, again):
                nonlocal tables
                settle()
                if again:
                    tell("dve_to_pool")
                    tell("dve_to_pe")
                tables += 1 if again else NT
                if again:
                    dve.wait_ge(kept_in, 16)
                else:
                    dve.wait_ge(table_in, 16 * tables)
                    hyena_filter()
                dve.wait_ge(pe_to_dve, heard.next("pe_to_dve"))
                for f in range(2):
                    zr, zi = bank(4 + f), bank(6 + f)
                    kr, ki, ka = KF[:, f, :], KF[:, 2 + f, :], KF[:, 4 if f == 0 else 1, :]
                    V.tensor_tensor(YF[:, f, :], zr, kr, ALU.mult)
                    V.tensor_tensor(TMP[:, 0, :], zi, ki, ALU.mult)
                    V.tensor_tensor(YF[:, 2 + f, :], zr, ki, ALU.mult)
                    V.tensor_tensor(TMP[:, 1, :], zi, ka, ALU.mult)
                    settle()
                    V.tensor_tensor(YF[:, f, :], YF[:, f, :], TMP[:, 0, :], ALU.subtract)
                    V.tensor_tensor(YF[:, 2 + f, :], YF[:, 2 + f, :], TMP[:, 1, :], ALU.add)
                    settle()
                tell("dve_to_pe")
                for c in range(4):
                    bias = PV[:, 3, 66 + 4 * l + c:67 + 4 * l + c]
                    V.tensor_scalar(U[:, c, :], U[:, c, :], bias, None, ALU.mult)
                settle()
                dve.wait_ge(pe_to_dve, heard.next("pe_to_dve"))
                for c in range(4):
                    V.scalar_tensor_tensor(U[:, 4 + c, :], W[:, c, 0:T], rn[:, c:c + 1], U[:, c, :], ALU.mult, ALU.add)
                settle()
                V.tensor_tensor(U[:, 4:8, :], U[:, 4:8, :], U[:, 8:12, :], ALU.mult)
                settle()

            def mix2(inst, full, l):
                x = inst[0] == "x"
                st = 0 if x else 1
                t0 = T if x else 0
                res = X if x else C
                norm(res, lambda k: GS[:, l, st, 0, k:k + 1], shift=lambda k: MOD[:, l, k, st:st + 1], hi=Hhi, lo=Hlo)

                def evac_in(n, b):
                    i = n - 6
                    w = lambda j: PV[:, 4, 36 * l + 12 * j + i:36 * l + 12 * j + i + 1]
                    bias = PV[:, 3, 42 + 12 * l + i:43 + 12 * l + i]
                    link(V.tensor_scalar(U[:, i, :], b[:, 0:T], w(1), bias, ALU.mult, ALU.add))
                    link(V.scalar_tensor_tensor(U[:, i, 1:T], b[:, 0:T - 1], w(0), U[:, i, 1:T], ALU.mult, ALU.add))
                    V.scalar_tensor_tensor(U[:, i, 0:T - 1], b[:, 1:T], w(2), U[:, i, 0:T - 1], ALU.mult, ALU.add
                                           ).then_inc(dve_to_pe, 1)

                linear(places2[inst + "in"], IN2(full), to_in2(full), evac_in)
                settle()
                if full:
                    V.tensor_tensor(U[:, 0:4, :], U[:, 0:4, :], U[:, 4:8, :], ALU.mult)
                dve.wait_ge(pe_to_dve, heard.next("pe_to_dve"))
                if x:
                    link(V.tensor_tensor(ROT[64:96, 0, :], W[64:96, 1, 0:T], mcos[64:96, :], ALU.mult))
                    link(V.tensor_tensor(ROT[64:96, 1, :], W[64:96, 2, 0:T], msin[64:96, :], ALU.mult))
                    link(V.tensor_tensor(ROT[64:96, 0, :], ROT[64:96, 0, :], ROT[64:96, 1, :], ALU.add))
                else:
                    link(V.tensor_copy(ROT[64:96, 0, :], W[64:96, 1, 0:T]))
                V.tensor_copy(KTt[64:96, :, t0:t0 + T], ROT[64:96, 0, :].unsqueeze(1).broadcast_to([32, 8, T]))
                if full:
                    norm(PQ, lambda k: PV[:, 3, 32 + 3 * l + k:33 + 3 * l + k], 3, hi=Ghi, lo=Glo, told=True)
                norm(PQ[:, 3:5, :], lambda k: PV[:, 3, 38 + 2 * l + k:39 + 2 * l + k], 2, hi=Ghi, lo=Glo, at=3, told=not full)
                linear(places2[inst + "qkv"], QKV(full), lambda n: "act", None)
                if not full:
                    return
                dve.wait_ge(weight_used, OFF + places2[inst + "qkv"].u + sizes2[inst + "qkv"])
                tell("dve_to_pool")
                if x:
                    dve.wait_ge(pe_to_dve, heard.next("pe_to_dve"))
                    for h in range(8):
                        rotate(TT[0:96, h, :], TT[0:96, h, :], W[0:96, h // 2, h % 2 * T:h % 2 * T + T], mcos[:, :],
                               msin[:, :], (S[0:96, 2816 + 512 * h:3072 + 512 * h], S[0:96, 3072 + 512 * h:3328 + 512 * h]))
                    tell("dve_to_pe")
                attention(512 if x else 256, PQ)
                hyena(l, inst == "x0")
                tell("dve_to_act")
                split_lo(PQ, 0, Ghi, Glo, 0, 4)
                split_lo(U, 4, Ghi, Glo, 4, 4).then_inc(dve_to_pe, 1)

                def evac_merge(n, b):
                    j = n // 4
                    if n % 4 == 2:
                        dve.wait_ge(act_to_dve, heard.next("act_to_dve"))
                        V.tensor_tensor(TT[:, j, :], PQ[:, (4, 2)[j % 2], :], b[:, 0:T], ALU.mult
                                        ).then_inc(dve_to_pe, 1)
                    else:
                        V.tensor_tensor(PQ[:, j % 2, :], PQ[:, (4, 2)[j % 2] + 1, :], b[:, 0:T], ALU.mult
                                        ).then_inc(dve_to_pe, 1)
                        settle()
                        V.tensor_tensor(TT[:, j, :], TT[:, j, :], PQ[:, j % 2, :], ALU.add)

                linear(places2[inst + "merge"], MERGE, to_merge, evac_merge)
                tell("dve_to_act")
                split_lo(TT, 0, Hhi, Hlo, 0, 8).then_inc(dve_to_pe, 1)

                def evac_out(n, b):
                    V.scalar_tensor_tensor(res[:, n, :], b[:, 0:T], MOD[:, l, 16 + n, st:st + 1], res[:, n, :],
                                           ALU.mult, ALU.add).then_inc(dve_to_act, 1)

                linear(places2[inst + "out"], [(KT, 128)] * KT, lambda n: "dve", evac_out)

            def select(q):
                link(V.tensor_copy(now[:, 0:4].unsqueeze(1), slots[:, bass.ds(q, 1), :]))
                for a in range(2):
                    ins = V.tensor_scalar(sel[:, a, :], kplan[:, 544:672], now[:, a:a + 1], None, ALU.is_equal)
                return ins

            def weigh_rows():
                link(V.tensor_scalar(Y, YP, now[:, 4:5], None, ALU.mult))
                tell("dve_to_act")

            def split_rows():
                dve.wait_ge(act_to_dve, heard.next("act_to_dve"))
                V.tensor_tensor(Ylo[:, :], Y, Yhi[:, :].bitcast(F32), ALU.subtract).then_inc(dve_to_pe, 1)

            def add_tiles(r):
                dve.wait_ge(pe_to_dve, heard.next("pe_to_dve"))
                for d in range(4 * r, 4 * r + 4):
                    ins = V.scalar_tensor_tensor(X[:, d, :], ACC[:, 4 + d % 4, :], MOD[:, 1, 40 + d, 0:1], X[:, d, :],
                                                 ALU.mult, ALU.add)
                return ins

            def item(p, i):
                at = {x: n for n, x in enumerate(ITEM)}
                upto = split_units(p, [1024] * FFU)

                def low(g):
                    dve.wait_ge(act_to_dve, heard.next("act_to_dve"))
                    V.tensor_tensor(hgo[:, g % 2, 0:GROUPS[g]], W[:, 2 * (g % 2), 0:GROUPS[g]],
                                    hgi[:, g % 2, 0:GROUPS[g]].bitcast(F32), ALU.subtract).then_inc(dve_to_pe, 1)

                upto(SPLIT - 1)
                dve.wait_ge(weight_used, OFF + p.u)
                weigh_rows()
                upto(SPLIT)
                split_rows()
                for g in range(NG):
                    parts = GROUPS[g] // 128
                    if g >= 1:
                        upto(at[("gate", g, parts - 1)] + SPLIT)
                        low(g - 1)
                    n = at[("up", g, parts - 1)]
                    upto(n + SPLIT)
                    dve.wait_ge(act_to_dve, heard.next("act_to_dve"))
                    dve.wait_ge(weight_used, OFF + p.u + n + 1)
                    V.tensor_tensor(hdt[:, g % 2, 0:GROUPS[g]], sgt[:, g % 2, 0:GROUPS[g]],
                                    W[:, 2 * (g % 2) + 1, 0:GROUPS[g]], ALU.mult).then_inc(dve_to_pe, 1)
                    if g in (1, 2):
                        add_tiles(g - 1).then_inc(dve_to_pe, 1)
                    if g == 3:
                        select(dve.value_load(plan[0:1, bass.ds(i + 1, 1)], min_val=0, max_val=ITEMS - 1)
                               ).then_inc(dve_to_pe, 1)
                upto(FFU)
                low(NG - 1)

            V.memset(ones[:, :], 1.0)
            V.memset(VP[:, :, 0:30], 0.0)
            V.memset(epsc, EPS)
            V.memset(small[0:1, 51:52], 0.0)
            V.memset(onec, 1.0)
            V.memset(zeroc, 0.0)
            V.memset(halfc, 0.5).then_inc(weight_split, OFF)
            tell("dve_to_pe")
            dve.wait_ge(pe_to_dve, heard.next("pe_to_dve"))
            V.tensor_copy(PV[:, 0:2, 0:94], W[:, 0, 0:256].rearrange("p (a n) -> p a n", a=2)[:, :, 0:94])
            V.tensor_copy(PV[:, 2, 0:96], W[:, 0, 256:352])
            V.tensor_copy(PV[:, 3, 0:106], W[:, 0, 384:490])
            V.tensor_copy(PV[:, 4, 0:72], W[:, 1, 0:72])
            tell("dve_to_pe")
            tell("dve_to_act")
            settle()
            dve.wait_ge(act_to_dve, heard.next("act_to_dve"))
            V.tensor_tensor(CS4[:, :, 2:4], CS[:, :, :], CS4[:, :, 0:2].bitcast(F32), ALU.subtract)
            settle()
            with dve.Fori(0, 2) as l:
                heard.enter("layers", l)
                p = places1(l)
                V.tensor_copy(PL[:, 0:94].unsqueeze(1), PV[:, bass.ds(l, 1), 0:94])
                V.tensor_copy(BL[:, :], PV[:, 2, bass.ds(l * 48, 48)])
                norm(X, lambda k: PL[:, k:k + 1], hi=Hhi, lo=Hlo)
                ffn(p["ffn1"], lambda n: 0.5, X, riders=0)
                norm(X, lambda k: PL[:, 8 + k:9 + k], hi=Hhi, lo=Hlo, told=True)
                mix1(p)
                norm(X, lambda k: PL[:, 16 + k:17 + k], hi=Hhi, lo=Hlo, told=True)
                ffn(p["ffn2"], lambda n: 0.5, X, riders=1, tiles=False)
                V.tensor_copy(MOD[:, bass.ds(l, 1), :, :].rearrange("p a n s -> p a (n s)"),
                              ML[:, :, :].rearrange("p n s -> p (n s)").unsqueeze(1))
                settle()
                heard.leave("layers", 2)
            for l in range(2):
                for st in range(2):
                    for w in range(2):
                        V.scalar_tensor_tensor(GS[:, l, st, w, :], MOD[:, l, 8 + 24 * w:16 + 24 * w, st], 1.0,
                                               PV[:, 3, 16 * w + 8 * l:16 * w + 8 * l + 8], ALU.add, ALU.mult)
            settle()
            norm(X, lambda k: PV[:, 3, 74 + k:75 + k], to=X)
            for inst, l, full in MIXES:
                if inst == "c1":
                    for name, st, res in (("ffx", 0, X), ("ffc", 1, C)):
                        norm(res, lambda k: GS[:, 0, st, 1, k:k + 1], shift=lambda k: MOD[:, 0, 24 + k, st:st + 1],
                             hi=Hhi, lo=Hlo, told=st == 0)
                        ffn(places2[name], lambda n: MOD[:, 0, 40 + n, st:st + 1], res, tiles=False)
                        settle()
                mix2(inst, full, l)
            norm(X, lambda k: GS[:, 1, 0, 1, k:k + 1], shift=lambda k: MOD[:, 1, 24 + k, 0:1], hi=Hhi, lo=Hlo, told=True)
            dve.wait_ge(pe_to_dve, heard.next("pe_to_dve"))
            L = route[:, 0, 0:16].rearrange("p (a e) -> p a e", a=2)
            EL = route[:, 1, 0:16].rearrange("p (a e) -> p a e", a=2)
            more = route[:, 2, 0:128].rearrange("p (a e f) -> p a e f", a=2, e=NE)
            same = route[:, 3, 0:128].rearrange("p (a e f) -> p a e f", a=2, e=NE)
            rank = route[:, 4, 0:16].rearrange("p (a e) -> p a e", a=2)
            link(V.tensor_copy(L, W[:, 0, 0:16].rearrange("p (a e) -> p a e", a=2)))
            tell("dve_to_pe")
            V.tensor_reduce(small[:, 0:2], L, AX.X, ALU.max)
            other = L.unsqueeze(2).broadcast_to([128, 2, NE, NE])
            own = L.unsqueeze(3).broadcast_to([128, 2, NE, NE])
            V.tensor_tensor(more, other, own, ALU.is_gt)
            V.tensor_tensor(same, other, own, ALU.is_equal)
            settle()
            V.tensor_tensor(EL, L, small[:, 0:2].unsqueeze(2).broadcast_to([128, 2, NE]), ALU.subtract
                            ).then_inc(dve_to_act, 1)
            link(V.tensor_tensor(same, same, earlier[:, :, :].unsqueeze(1).broadcast_to([128, 2, NE, NE]), ALU.mult))
            link(V.tensor_tensor(more, more, same, ALU.add))
            link(V.tensor_reduce(rank, more, AX.X, ALU.add))
            link(V.tensor_scalar(rank, rank, TOP_K - 0.5, None, ALU.is_lt))
            dve.wait_ge(act_to_dve, heard.next("act_to_dve"))
            link(V.tensor_tensor(EL, EL, rank, ALU.mult))
            link(V.tensor_reduce(small[:, 2:4], EL, AX.X, ALU.add))
            link(V.reciprocal(small[:, 2:4], small[:, 2:4]))
            link(V.tensor_tensor(EL, EL, small[:, 2:4].unsqueeze(2).broadcast_to([128, 2, NE]), ALU.mult))
            tell("dve_to_pe")
            dve.wait_ge(pe_to_dve, heard.next("pe_to_dve"))
            for c in range(2):
                e8 = slice(NE * c, NE * c + NE)
                for a in range(2):
                    link(V.tensor_scalar(slots[:, e8, a], W[:, 0, 8 * a:8 * a + 8], 1.0 - 128 * c, None, ALU.add))
                    link(V.tensor_tensor(slots[:, e8, a], slots[:, e8, a], rank[:, a, :], ALU.mult))
                    link(V.tensor_scalar(slots[:, e8, a], slots[:, e8, a], 1.0, None, ALU.subtract))
                    V.tensor_copy(slots[:, e8, 2 + a], EL[:, a, :])
            active, before, row = route[:, 5, 0:16], route[:, 5, 16:32], route[:, 5, 32:48]
            for c in range(2):
                V.tensor_scalar(active[:, NE * c:NE * c + NE], W[:, 0, 16:24], 128 * c + 0.5, None, ALU.is_gt)
            settle()
            square = lambda v: v.rearrange("p (a b) -> p a b", a=16)
            m1, m2 = square(route[:, 2, :]), square(route[:, 3, :])
            link(V.tensor_tensor(m1, square(kplan[:, 0:256]), active.unsqueeze(1).broadcast_to([128, 16, 16]), ALU.mult))
            link(V.tensor_reduce(before, m1, AX.X, ALU.add))
            link(V.tensor_tensor(m1, square(kplan[:, 256:512]), before.unsqueeze(1).broadcast_to([128, 16, 16]), ALU.is_equal))
            link(V.tensor_tensor(m1, m1, active.unsqueeze(1).broadcast_to([128, 16, 16]), ALU.mult))
            for n in range(2):
                link(V.tensor_tensor(m2, m1, kplan[:, 512 + 16 * n:528 + 16 * n].unsqueeze(1).broadcast_to([128, 16, 16]),
                                     ALU.mult))
                link(V.tensor_reduce(row, m2, AX.X, ALU.add))
                link(V.tensor_copy(plan[:, 16 * n:16 * n + 16], row))
            link(V.tensor_reduce(row[:, 0:1], active, AX.X, ALU.add))
            link(V.tensor_copy(plan[:, 32:33], row[:, 0:1]))
            V.memset(now[:, 4:5], 0.0)
            V.memset(selT[:, :].bitcast(F32), 0.0).then_inc(plan_ready, 1)
            link(select(dve.value_load(plan[0:1, 0:1], min_val=0, max_val=ITEMS - 1)))
            tell("dve_to_pe")
            dve.wait_ge(pe_to_dve, heard.next("pe_to_dve"))
            n_items = dve.value_load(plan[0:1, 32:33], min_val=1, max_val=ITEMS)
            with dve.Fori(0, n_items) as i:
                heard.enter("items", i)
                item(place_moe(i), i)
                settle()
                heard.leave("items", n_items)
            dve.wait_ge(weight_used, OFF + place_moe(n_items).u)
            weigh_rows()
            split_rows()
            add_tiles(0).then_inc(dve_to_pe, 1)
            add_tiles(1)
            settle()
            norm(X, lambda k: PV[:, 3, 82 + k:83 + k])
            tell("dve_to_pe")


def tables():
    f = np.float32
    i = np.arange(128)
    t = np.arange(T)
    ident = np.eye(128)
    tri = (i[:, None] > i[None, :]) * 1.0
    blk = (i[:, None] // 64 == i[None, :] // 64) / 64.0
    perm64 = np.zeros((128, 128))
    for o in range(128):
        h, r = o // 64 * 64, o % 64
        perm64[h + (r + 32) % 64, o] = 1.0
    half = np.arange(32)
    ang = t[None, :].astype(f) * (1.0 / (f(10000.0) ** (half.astype(f) / f(32)))).astype(f)[:, None]
    rc, rs = np.cos(ang.astype(np.float64)), np.sin(ang.astype(np.float64))
    ret = np.concatenate([np.tile(rc, (4, 1)), np.tile(np.concatenate([-rs, rs]), (2, 1))], axis=1)
    perm96, selk = np.zeros((96, 96)), np.zeros((128, 2, 96))
    for r in range(32):
        perm96[64 + (r + 16) % 32, 64 + r] = 1.0
        selk[96 + r, 0, 64 + r] = 1.0
        selk[96 + (r + 16) % 32, 1, 64 + r] = 1.0
    n_freq = 8
    inv = (f(10000.0) ** (-np.arange(n_freq, dtype=f) / f(n_freq))).astype(f)
    a = np.concatenate([(t // 64).astype(f)[:, None] * inv, (t % 64).astype(f)[:, None] * inv], axis=-1).T
    mc, ms = np.cos(a.astype(np.float64)), np.sin(a.astype(np.float64))
    mcos = np.concatenate([np.ones((64, T)), mc, mc])
    msin = np.concatenate([np.zeros((64, T)), -ms, ms])
    diag = (i[:, None] < i[None, :]) * 1.0
    mask = np.concatenate([diag, np.ones((128, 128)), diag], axis=1)
    log_gamma = np.log1p(-np.exp2(-5.0 - np.arange(4)))
    s = t[:, None]
    full = np.exp(log_gamma[:, None, None] * np.abs(t[None, None, :] - s)) * (s // 64 <= t[None, :] // 64) * 0.125
    decay = np.concatenate([full[:, 0:128, :], full[:, 128:, 128:]], axis=2).transpose(1, 0, 2)
    w = 2 * np.pi * np.outer(t, t) / (2 * T)
    c, sn, alt = np.cos(w), -np.sin(w), (-1.0) ** t
    sn[:, 0] = 0.0
    snn, cn = sn.copy(), c[:, 0:128].copy()
    snn[:, 0], cn[:, 0] = alt, alt
    gc = np.cos(w) * 2 / (2 * T)
    gc[0] /= 2
    gs = -np.sin(w) * 2 / (2 * T)
    gs[0] = alt / (2 * T)
    tiles = lambda v: v.reshape(-1, 128, v.shape[1]).transpose(1, 0, 2).reshape(128, -1)
    dft = np.concatenate([tiles(c), tiles(snn), tiles(sn), tiles(cn), tiles(np.concatenate([gc, gs]))], axis=1)
    tl = np.linspace(0.0, 1.0, T, dtype=f)
    ph = (f(2.0 * math.pi / T) * t.astype(f))[:, None] * np.linspace(1e-4, 7, 8, dtype=f)
    hyz = np.concatenate([tl[:, None], np.cos(ph.astype(np.float64)), -np.sin(ph.astype(np.float64))], axis=-1).T
    earlier = np.broadcast_to((np.arange(NE)[:, None] > np.arange(NE)[None, :]) * 1.0, (128, NE, NE))
    q = np.arange(16)
    lists = [(q[None, :] < q[:, None]) * 1.0, np.broadcast_to(q[:, None], (16, 16)), q, q % NE, np.arange(128)]
    plan = np.broadcast_to(np.concatenate([v.ravel() for v in lists]), (128, 672))
    got = dict(k_plan=plan, k_ident=ident, k_tri=tri, k_blk=blk, k_perm64=perm64, k_perm96=perm96, k_selk=selk, k_mask=mask,
               k_mcos=mcos, k_msin=msin, k_ret=ret, k_decay=decay.reshape(128, -1), k_dft=dft, k_hyz=hyz,
               k_negt=-tl.reshape(2, 128).T, k_earlier=earlier)
    return {k: np.ascontiguousarray(v, dtype=f) for k, v in got.items()}


def kernel(**inputs):
    import concourse.bacc as bacc
    from concourse.bass_utils import run_bass_kernel_spmd

    nc = bacc.Bacc("TRN2", target_bir_lowering=False, num_devices=1)
    arrays, A = {}, {}
    for name, a in [*inputs.items(), *tables().items()]:
        a = np.ascontiguousarray(a)
        arrays[f"in_{name}"] = a
        A[name] = nc.dram_tensor(f"in_{name}", a.shape, mybir.dt.from_np(a.dtype), kind="ExternalInput").ap()
    out = nc.dram_tensor("out_0", (1, T, D), F32, kind="ExternalOutput").ap()
    nc.disable_value_cache = True
    program(nc, A, out)
    r = run_bass_kernel_spmd(nc, [arrays], core_ids=[0])
    return r.results[0]["out_0"]
```
